# Optimizing a Trainium2 kernel written in Bass

```python
import jax, jax.numpy as jnp
from jax import lax
import numpy as np
import math

D_MODEL = 2048
BATCH = 1
SEQ = 256
DEPTH = 1

HEAD_DIM = 64
Q_BLOCK = 128
A_GROUPS = ((128, 1), (512, 4), (2048, 16))
A_HEADS_PER_GROUP = 4
A_HEADS = A_HEADS_PER_GROUP * len(A_GROUPS)
B_HEADS = 8
B_KV_HEADS = 2
B_WINDOW = 128
C_HEADS = 12
C_KV_HEADS = 2
CMP_BLOCK = 32
CMP_STRIDE = 16
CMP_HIDDEN = 256
SLC_BLOCK = 64
SLC_TOPK = 16
C_WINDOW = 512
N_BRANCHES = 3
D_FF = 5632
RMS_EPS = 1e-6
NEG_INF = -1e30

A_OUT = A_HEADS_PER_GROUP * HEAD_DIM
B_OUT = B_HEADS * HEAD_DIM
C_OUT = C_HEADS * HEAD_DIM
A_QKV_COLS = 3 * A_HEADS * HEAD_DIM
B_Q_COLS = B_HEADS * HEAD_DIM
B_KV_COLS = 2 * B_KV_HEADS * HEAD_DIM
C_Q_COLS = C_HEADS * HEAD_DIM
C_KV_COLS = 6 * C_KV_HEADS * HEAD_DIM
C_GATE_COLS = 3 * C_HEADS
GATE_COLS = N_BRANCHES * D_MODEL
IN_COLS = A_QKV_COLS + B_Q_COLS + B_KV_COLS + C_Q_COLS + C_KV_COLS + C_GATE_COLS + GATE_COLS


def _rmsnorm(x, g):
    xf = x.astype(jnp.float32)
    y = xf * lax.rsqrt(jnp.mean(xf * xf, axis=-1, keepdims=True) + RMS_EPS)
    return (y * g.astype(jnp.float32)).astype(x.dtype)

def _alibi_slopes(n_heads):
    return jnp.asarray(2.0 ** (-8.0 * np.arange(1, n_heads + 1, dtype=np.float32) / n_heads), dtype=jnp.float32)

def _swiglu(h, w_gu, w_down):
    gate, up = jnp.split(h @ w_gu, 2, axis=-1)
    return (jax.nn.silu(gate) * up) @ w_down

def _masked_softmax(s, mask, sinks=None, with_lse=False):
    s = jnp.where(mask, s, NEG_INF)
    m = jnp.max(s, axis=-1, keepdims=True)
    if sinks is not None:
        m = jnp.maximum(m, sinks)
    e = jnp.where(mask, jnp.exp(s - m), 0.0)
    den = jnp.sum(e, axis=-1, keepdims=True)
    if sinks is not None:
        den = den + jnp.exp(sinks - m)
    p = e / jnp.where(den > 0, den, 1.0)
    if with_lse:
        return p, (m + jnp.log(den))[..., 0]
    return p

def _banded_attention(q, k, v, max_dist, slopes, dist_scale, sinks=None, with_lse=False):
    n, length, g, r, dh = q.shape
    nb = -(-max_dist // Q_BLOCK)
    nq = -(-length // Q_BLOCK)
    pad = nq * Q_BLOCK - length
    nk = (nb + 1) * Q_BLOCK
    q = jnp.pad(q, ((0, 0), (0, pad), (0, 0), (0, 0), (0, 0)))
    kv_pad = ((0, 0), (nb * Q_BLOCK, pad), (0, 0), (0, 0))
    k = jnp.pad(k, kv_pad)
    v = jnp.pad(v, kv_pad)
    rel = nb * Q_BLOCK + jnp.arange(Q_BLOCK)[:, None] - jnp.arange(nk)[None, :]
    band = (rel >= 0) & (rel <= max_dist)
    bias = -(slopes * dist_scale)[:, :, None, None] * rel.astype(jnp.float32)
    sink_logits = None if sinks is None else sinks[:, :, None, None].astype(jnp.float32)
    scale = dh ** -0.5

    def one_block(i):
        qb = lax.dynamic_slice_in_dim(q, i * Q_BLOCK, Q_BLOCK, axis=1)
        kb = lax.dynamic_slice_in_dim(k, i * Q_BLOCK, nk, axis=1)
        vb = lax.dynamic_slice_in_dim(v, i * Q_BLOCK, nk, axis=1)
        s = jnp.einsum('nqgrd,nkgd->ngrqk', qb, kb).astype(jnp.float32) * scale + bias
        key_pos = (i - nb) * Q_BLOCK + jnp.arange(nk)
        mask = band & (key_pos >= 0)[None, :]
        if with_lse:
            p, lse = _masked_softmax(s, mask, sink_logits, True)
            return jnp.einsum('ngrqk,nkgd->nqgrd', p.astype(vb.dtype), vb), lse
        p = _masked_softmax(s, mask, sink_logits)
        return jnp.einsum('ngrqk,nkgd->nqgrd', p.astype(vb.dtype), vb)

    res = lax.map(one_block, jnp.arange(nq))
    o = res[0] if with_lse else res
    o = jnp.moveaxis(o, 0, 1).reshape(n, nq * Q_BLOCK, g, r, dh)[:, :length]
    if with_lse:
        lse = res[1].transpose(1, 0, 4, 2, 3).reshape(n, nq * Q_BLOCK, g, r)[:, :length]
        return o, lse
    return o

def _dilated_mixer(q, k, v, slopes):
    b, s, _, dh = q.shape
    hpg = A_HEADS_PER_GROUP
    outs, lses = [], []
    for gi, (window, dil) in enumerate(A_GROUPS):
        hs = slice(gi * hpg, (gi + 1) * hpg)

        def to_strided(t):
            return t.reshape(b, s // dil, dil, hpg, dh).transpose(0, 2, 1, 3, 4).reshape(b * dil, s // dil, hpg, dh)

        o, lse = _banded_attention(to_strided(q[:, :, hs])[:, :, :, None], to_strided(k[:, :, hs]),
                                   to_strided(v[:, :, hs]), window // dil, slopes[hs][:, None], dil,
                                   with_lse=True)
        outs.append(o.reshape(b, dil, s // dil, hpg, dh).transpose(0, 2, 1, 3, 4).reshape(b, s, hpg, dh))
        lses.append(lse.reshape(b, dil, s // dil, hpg).transpose(0, 2, 1, 3).reshape(b, s, hpg))
    w = jax.nn.softmax(jnp.stack(lses), axis=0)
    o = jnp.einsum('gbsh,gbshd->bshd', w.astype(q.dtype), jnp.stack(outs))
    return o.reshape(b, s, hpg * dh)

def _sink_swa_mixer(q, k, v, slopes, sinks):
    b, s, _, dh = q.shape
    r = B_HEADS // B_KV_HEADS
    o = _banded_attention(q.reshape(b, s, B_KV_HEADS, r, dh), k, v, B_WINDOW - 1,
                          slopes.reshape(B_KV_HEADS, r), 1, sinks=sinks.reshape(B_KV_HEADS, r))
    return o.reshape(b, s, B_OUT)

def _compress(t, pos, w1, w2):
    b, s, g, dh = t.shape
    n_cmp = (s - CMP_BLOCK) // CMP_STRIDE + 1
    idx = CMP_STRIDE * jnp.arange(n_cmp)[:, None] + jnp.arange(CMP_BLOCK)[None, :]
    blocks = t[:, idx] + pos[None, None, :, None, :]
    blocks = blocks.transpose(0, 1, 3, 2, 4).reshape(b, n_cmp, g, CMP_BLOCK * dh)
    return jax.nn.silu(blocks @ w1) @ w2

def _nsa_mixer(q, k_cmp, v_cmp, k_slc, v_slc, k_win, v_win, gate_logits, slopes, q_gain, k_gain,
               cmp_pos, cmp_w1, cmp_w2):
    b, s, _, dh = q.shape
    g = C_KV_HEADS
    r = C_HEADS // g
    scale = dh ** -0.5
    q = _rmsnorm(q, q_gain).reshape(b, s, g, r, dh)
    slopes = slopes.reshape(g, r)
    sl = slopes[None, :, :, None, None]
    kc = _rmsnorm(_compress(k_cmp, cmp_pos[0], cmp_w1[0], cmp_w2[0]), k_gain)
    vc = _compress(v_cmp, cmp_pos[1], cmp_w1[1], cmp_w2[1])
    n_cmp = kc.shape[1]
    cmp_start = CMP_STRIDE * jnp.arange(n_cmp)
    cmp_end = cmp_start + CMP_BLOCK - 1
    n_slc = s // SLC_BLOCK
    slc_start = SLC_BLOCK * jnp.arange(n_slc)
    overlap = ((cmp_start[:, None] <= slc_start[None, :] + SLC_BLOCK - 1)
               & (cmp_end[:, None] >= slc_start[None, :])).astype(jnp.float32)
    n_top = min(SLC_TOPK, n_slc)
    k_slc = _rmsnorm(k_slc, k_gain)
    ks_blk = k_slc.reshape(b, n_slc, SLC_BLOCK, g, dh).transpose(0, 3, 1, 2, 4)
    vs_blk = v_slc.reshape(b, n_slc, SLC_BLOCK, g, dh).transpose(0, 3, 1, 2, 4)
    bi = jnp.arange(b)[:, None, None, None]
    gi = jnp.arange(g)[None, :, None, None]
    n_keys = n_top * SLC_BLOCK

    def one_block(i):
        qb = lax.dynamic_slice_in_dim(q, i * Q_BLOCK, Q_BLOCK, axis=1)
        t = i * Q_BLOCK + jnp.arange(Q_BLOCK)
        d_cmp = (t[:, None] - cmp_end[None, :]).astype(jnp.float32)
        s_cmp = jnp.einsum('bqgrd,bngd->bgrqn', qb, kc).astype(jnp.float32) * scale - sl * d_cmp
        p_cmp = _masked_softmax(s_cmp, d_cmp >= 0)
        o_cmp = jnp.einsum('bgrqn,bngd->bqgrd', p_cmp.astype(vc.dtype), vc)
        imp = jnp.einsum('bgrqn,nj->bgqj', p_cmp, overlap)
        cur = (t // SLC_BLOCK)[:, None]
        j = jnp.arange(n_slc)[None, :]
        forced = (j == 0) | (j == cur) | (j == cur - 1)
        imp = jnp.where(j <= cur, jnp.where(forced, jnp.inf, imp), -jnp.inf)
        _, sel = lax.top_k(imp, n_top)
        kg = ks_blk[bi, gi, sel].reshape(b, g, Q_BLOCK, n_keys, dh)
        vg = vs_blk[bi, gi, sel].reshape(b, g, Q_BLOCK, n_keys, dh)
        key_pos = sel[..., None] * SLC_BLOCK + jnp.arange(SLC_BLOCK)
        d_slc = (t[:, None, None] - key_pos).reshape(b, g, Q_BLOCK, n_keys).astype(jnp.float32)[:, :, None]
        s_slc = jnp.einsum('bqgrd,bgqkd->bgrqk', qb, kg).astype(jnp.float32) * scale - sl * d_slc
        p_slc = _masked_softmax(s_slc, d_slc >= 0)
        o_slc = jnp.einsum('bgrqk,bgqkd->bqgrd', p_slc.astype(vg.dtype), vg)
        return o_cmp, o_slc

    o_cmp, o_slc = lax.map(one_block, jnp.arange(s // Q_BLOCK))
    o_cmp = jnp.moveaxis(o_cmp, 0, 1).reshape(b, s, g, r, dh)
    o_slc = jnp.moveaxis(o_slc, 0, 1).reshape(b, s, g, r, dh)
    o_win = _banded_attention(q, _rmsnorm(k_win, k_gain), v_win, C_WINDOW - 1, slopes, 1)
    gate = jax.nn.sigmoid(gate_logits.astype(jnp.float32)).astype(q.dtype).reshape(b, s, g, r, 3)
    o = gate[..., 0:1] * o_cmp + gate[..., 1:2] * o_slc + gate[..., 2:3] * o_win
    return o.reshape(b, s, C_OUT)

def _token_mixing(h, w_in, qk_gain, sinks, cmp_pos, cmp_w1, cmp_w2, w_branch_a, w_branch_b, w_branch_c, w_out):
    b, s, _ = h.shape
    dh = HEAD_DIM
    proj = h @ w_in
    offs, acc = [], 0
    for width in (A_QKV_COLS, B_Q_COLS, B_KV_COLS, C_Q_COLS, C_KV_COLS, C_GATE_COLS):
        acc += width
        offs.append(acc)
    a_qkv, b_q, b_kv, c_q, c_kv, c_gate, br_gate = jnp.split(proj, offs, axis=-1)
    a_qkv = a_qkv.reshape(b, s, 3, A_HEADS, dh)
    o_a = _dilated_mixer(_rmsnorm(a_qkv[:, :, 0], qk_gain[0, 0]), _rmsnorm(a_qkv[:, :, 1], qk_gain[0, 1]),
                         a_qkv[:, :, 2], _alibi_slopes(A_HEADS))
    b_kv = b_kv.reshape(b, s, 2, B_KV_HEADS, dh)
    o_b = _sink_swa_mixer(_rmsnorm(b_q.reshape(b, s, B_HEADS, dh), qk_gain[1, 0]),
                          _rmsnorm(b_kv[:, :, 0], qk_gain[1, 1]), b_kv[:, :, 1], _alibi_slopes(B_HEADS), sinks)
    c_kv = c_kv.reshape(b, s, 6, C_KV_HEADS, dh)
    o_c = _nsa_mixer(c_q.reshape(b, s, C_HEADS, dh), c_kv[:, :, 0], c_kv[:, :, 1], c_kv[:, :, 2], c_kv[:, :, 3],
                     c_kv[:, :, 4], c_kv[:, :, 5], c_gate, _alibi_slopes(C_HEADS), qk_gain[2, 0], qk_gain[2, 1],
                     cmp_pos, cmp_w1, cmp_w2)
    gates = jax.nn.sigmoid(br_gate.astype(jnp.float32)).astype(h.dtype).reshape(b, s, N_BRANCHES, D_MODEL)
    merged = (gates[:, :, 0] * (o_a @ w_branch_a) + gates[:, :, 1] * (o_b @ w_branch_b)
              + gates[:, :, 2] * (o_c @ w_branch_c))
    return merged @ w_out

def first_inputs(seed: int = 0) -> dict:
    key = jax.random.key(seed)
    ks = jax.random.split(key, 18)
    f32 = jnp.float32

    def dense(k, shape, fan_in):
        return jax.random.normal(k, shape, f32) * (fan_in ** -0.5)

    def gain(k, shape):
        return 1.0 + 0.05 * jax.random.normal(k, shape, f32)

    return {
        'x': jax.random.normal(ks[0], (BATCH, SEQ, D_MODEL), f32),
        'ffn1_norm': gain(ks[1], (DEPTH, D_MODEL)),
        'ffn1_w_gu': dense(ks[2], (DEPTH, D_MODEL, 2 * D_FF), D_MODEL),
        'ffn1_w_down': dense(ks[3], (DEPTH, D_FF, D_MODEL), D_FF),
        'mix_norm': gain(ks[4], (DEPTH, D_MODEL)),
        'w_in': dense(ks[5], (DEPTH, D_MODEL, IN_COLS), D_MODEL),
        'qk_gain': gain(ks[6], (DEPTH, 3, 2, HEAD_DIM)),
        'sinks': 0.5 * jax.random.normal(ks[7], (DEPTH, B_HEADS), f32),
        'cmp_pos': 0.02 * jax.random.normal(ks[8], (DEPTH, 2, CMP_BLOCK, HEAD_DIM), f32),
        'cmp_w1': dense(ks[9], (DEPTH, 2, CMP_BLOCK * HEAD_DIM, CMP_HIDDEN), CMP_BLOCK * HEAD_DIM),
        'cmp_w2': dense(ks[10], (DEPTH, 2, CMP_HIDDEN, HEAD_DIM), CMP_HIDDEN),
        'w_branch_a': dense(ks[11], (DEPTH, A_OUT, D_MODEL), A_OUT),
        'w_branch_b': dense(ks[12], (DEPTH, B_OUT, D_MODEL), B_OUT),
        'w_branch_c': dense(ks[13], (DEPTH, C_OUT, D_MODEL), C_OUT),
        'w_out': dense(ks[14], (DEPTH, D_MODEL, D_MODEL), D_MODEL),
        'ffn2_norm': gain(ks[15], (DEPTH, D_MODEL)),
        'ffn2_w_gu': dense(ks[16], (DEPTH, D_MODEL, 2 * D_FF), D_MODEL),
        'ffn2_w_down': dense(ks[17], (DEPTH, D_FF, D_MODEL), D_FF),
    }

def first_block(x, ffn1_norm, ffn1_w_gu, ffn1_w_down, mix_norm, w_in, qk_gain, sinks, cmp_pos, cmp_w1, cmp_w2,
              w_branch_a, w_branch_b, w_branch_c, w_out, ffn2_norm, ffn2_w_gu, ffn2_w_down):
    for l in range(DEPTH):
        x = x + 0.5 * _swiglu(_rmsnorm(x, ffn1_norm[l]), ffn1_w_gu[l], ffn1_w_down[l])
        x = x + _token_mixing(_rmsnorm(x, mix_norm[l]), w_in[l], qk_gain[l], sinks[l], cmp_pos[l], cmp_w1[l],
                              cmp_w2[l], w_branch_a[l], w_branch_b[l], w_branch_c[l], w_out[l])
        x = x + 0.5 * _swiglu(_rmsnorm(x, ffn2_norm[l]), ffn2_w_gu[l], ffn2_w_down[l])
    return x


DEPTH_2 = 2

GRID_W = 64
D_MIX = D_MODEL
N_MIXERS = 4
D_GROUP = D_MIX // N_MIXERS
N_NA_HEADS = D_GROUP // HEAD_DIM
N_RET_HEADS = D_GROUP // HEAD_DIM
N_FFT_GROUPS = 4
FFT_GROUP_DIM = D_GROUP // N_FFT_GROUPS
NA_KH_MAX = 8
NA_KW = 16
RET_CHUNK = 128
CONV_WIDTH = 31
ROPE_BASE = 10000.0
EPS = 1e-6
N_IN_PIECES = 13
D_IN = N_IN_PIECES * D_GROUP


def _rmsnorm_2(x, g):
    xf = x.astype(jnp.float32)
    ms = jnp.mean(xf * xf, axis=-1, keepdims=True)
    return (xf * lax.rsqrt(ms + EPS)).astype(x.dtype) * g

def _fourier_mix(u, w_fft):
    B, S, _ = u.shape
    uf = u.astype(jnp.float32).reshape(B, S, N_FFT_GROUPS, FFT_GROUP_DIM)
    y = jnp.real(jnp.fft.fft2(uf, axes=(1, 3), norm="ortho"))
    return y.reshape(B, S, D_GROUP).astype(u.dtype) @ w_fft

def _neighbourhood_attention(q, k, v, rel_bias):
    B, S, _ = q.shape
    rows = S // GRID_W
    kh = min(NA_KH_MAX, rows)

    def grid(t):
        return t.reshape(B, rows, GRID_W, N_NA_HEADS, HEAD_DIM)

    qg = grid(q) * (HEAD_DIM ** -0.5)
    kg, vg = grid(k), grid(v)
    r = jnp.arange(rows)
    row_start = jnp.clip(r - kh // 2, 0, rows - kh)
    key_rows = row_start[:, None] + jnp.arange(kh)[None, :]
    kb = kg[:, key_rows]
    vb = vg[:, key_rows]
    col = jnp.arange(GRID_W)
    col_start = jnp.clip(col - NA_KW // 2, 0, GRID_W - NA_KW)
    rel_c = col[None, :] - col_start[:, None]
    col_in = (rel_c >= 0) & (rel_c < NA_KW)
    dc = col[None, :] - col[:, None]
    dr = key_rows - r[:, None]
    bias = rel_bias[:, (dr + NA_KH_MAX - 1)[:, :, None, None],
                    jnp.clip(dc + NA_KW - 1, 0, 2 * NA_KW - 2)[None, None]]
    bias = bias.transpose(0, 1, 3, 2, 4)
    s = jnp.einsum('brqhd,brakhd->bhrqak', qg, kb).astype(jnp.float32)
    s = s + bias[None].astype(jnp.float32)
    s = jnp.where(col_in[:, None, :], s, -jnp.inf)
    p = jax.nn.softmax(s.reshape(B, N_NA_HEADS, rows, GRID_W, kh * GRID_W), axis=-1)
    p = p.reshape(B, N_NA_HEADS, rows, GRID_W, kh, GRID_W).astype(v.dtype)
    o = jnp.einsum('bhrqak,brakhd->brqhd', p, vb)
    return o.reshape(B, S, D_GROUP)

def _rotary(t):
    S = t.shape[2]
    half = HEAD_DIM // 2
    inv = ROPE_BASE ** (-jnp.arange(half, dtype=jnp.float32) / half)
    ang = jnp.arange(S, dtype=jnp.float32)[:, None] * inv[None, :]
    cos, sin = jnp.cos(ang), jnp.sin(ang)
    t1, t2 = t[..., :half], t[..., half:]
    return jnp.concatenate([t1 * cos - t2 * sin, t1 * sin + t2 * cos], axis=-1)

def _retention_direction(q, k, v, log_gamma, include_diag):
    B, H, S, Dh = q.shape
    C = RET_CHUNK
    n = S // C
    qc = q.reshape(B, H, n, C, Dh)
    kc = k.reshape(B, H, n, C, Dh)
    vc = v.reshape(B, H, n, C, Dh)
    idx = jnp.arange(C, dtype=jnp.float32)
    diff = idx[:, None] - idx[None, :]
    mask = (diff >= 0) if include_diag else (diff > 0)
    lg = log_gamma[:, None, None]
    d_intra = jnp.where(mask, jnp.exp(lg * jnp.where(mask, diff, 0.0)), 0.0)
    scores = jnp.einsum('bhnid,bhnjd->bhnij', qc, kc) * d_intra[None, :, None]
    o_intra = jnp.einsum('bhnij,bhnjd->bhnid', scores, vc)
    k_decay = jnp.exp(log_gamma[:, None] * (C - 1 - idx)[None, :])
    kv = jnp.einsum('bhnjd,bhnje->nbhde', kc * k_decay[None, :, None, :, None], vc)
    chunk_decay = jnp.exp(log_gamma * C)[None, :, None, None]

    def step(state, kv_n):
        return chunk_decay * state + kv_n, state

    _, prev = lax.scan(step, jnp.zeros((B, H, Dh, Dh), jnp.float32), kv)
    q_decay = jnp.exp(log_gamma[:, None] * (idx + 1.0)[None, :])
    o_cross = jnp.einsum('bhnid,nbhde->bhnie', qc * q_decay[None, :, None, :, None], prev)
    return (o_intra + o_cross).reshape(B, H, S, Dh)

def _retention(q, k, v, logit_fwd, logit_bwd):
    B, S, _ = q.shape

    def heads(t):
        return t.astype(jnp.float32).reshape(B, S, N_RET_HEADS, HEAD_DIM).transpose(0, 2, 1, 3)

    qh = _rotary(heads(q)) * (HEAD_DIM ** -0.5)
    kh = _rotary(heads(k))
    vh = heads(v)
    lf = jax.nn.log_sigmoid(logit_fwd.astype(jnp.float32))
    lb = jax.nn.log_sigmoid(logit_bwd.astype(jnp.float32))
    fwd = _retention_direction(qh, kh, vh, lf, True)
    bwd = _retention_direction(qh[:, :, ::-1], kh[:, :, ::-1], vh[:, :, ::-1], lb, False)[:, :, ::-1]
    o = fwd + bwd
    o = o * lax.rsqrt(jnp.mean(o * o, axis=-1, keepdims=True) + EPS)
    return o.transpose(0, 2, 1, 3).reshape(B, S, D_GROUP).astype(q.dtype)

def _conformer_conv(a, b, conv_w, conv_b, ln_g, ln_b, w_pw):
    u = a * jax.nn.sigmoid(b)
    y = lax.conv_general_dilated(
        u, conv_w[:, None, :].astype(u.dtype), window_strides=(1,),
        padding=[(CONV_WIDTH // 2, CONV_WIDTH // 2)],
        dimension_numbers=('NWC', 'WIO', 'NWC'), feature_group_count=D_GROUP) + conv_b
    yf = y.astype(jnp.float32)
    mu = jnp.mean(yf, axis=-1, keepdims=True)
    var = jnp.mean((yf - mu) ** 2, axis=-1, keepdims=True)
    y = ((yf - mu) * lax.rsqrt(var + EPS)).astype(u.dtype) * ln_g + ln_b
    return jax.nn.silu(y) @ w_pw

def second_inputs(seed: int = 0) -> dict:
    key = jax.random.key(seed)
    ks = jax.random.split(key, 17)
    f32 = jnp.float32
    nrm = lambda k, shape, s: jax.random.normal(k, shape, f32) * s
    gam = 1.0 - 2.0 ** (-5.0 - jnp.arange(N_RET_HEADS, dtype=f32))
    ret_logit0 = jnp.log(gam) - jnp.log1p(-gam)
    return {
        "x": nrm(ks[0], (BATCH, SEQ, D_MODEL), 1.0),
        "c": nrm(ks[1], (BATCH, D_MODEL), 1.0),
        "norm_g": 1.0 + nrm(ks[2], (DEPTH_2, D_MODEL), 0.01),
        "w_ada": nrm(ks[3], (DEPTH_2, D_MODEL, 3 * D_MODEL), 0.5 * D_MODEL ** -0.5),
        "b_ada": nrm(ks[4], (DEPTH_2, 3 * D_MODEL), 0.01),
        "w_in": nrm(ks[5], (DEPTH_2, D_MODEL, D_IN), D_MODEL ** -0.5),
        "w_fft": nrm(ks[6], (DEPTH_2, D_GROUP, D_GROUP), D_GROUP ** -0.5),
        "na_rel_bias": nrm(ks[7], (DEPTH_2, N_NA_HEADS, 2 * NA_KH_MAX - 1, 2 * NA_KW - 1), 0.02),
        "ret_logit_fwd": ret_logit0[None] + nrm(ks[8], (DEPTH_2, N_RET_HEADS), 0.01),
        "ret_logit_bwd": ret_logit0[None] + nrm(ks[9], (DEPTH_2, N_RET_HEADS), 0.01),
        "conv_w": nrm(ks[10], (DEPTH_2, CONV_WIDTH, D_GROUP), CONV_WIDTH ** -0.5),
        "conv_b": nrm(ks[11], (DEPTH_2, D_GROUP), 0.01),
        "conv_ln_g": 1.0 + nrm(ks[12], (DEPTH_2, D_GROUP), 0.01),
        "conv_ln_b": nrm(ks[13], (DEPTH_2, D_GROUP), 0.01),
        "conv_w_pw": nrm(ks[14], (DEPTH_2, D_GROUP, D_GROUP), D_GROUP ** -0.5),
        "w_out": nrm(ks[15], (DEPTH_2, D_MIX, D_MODEL), D_MIX ** -0.5),
        "final_g": 1.0 + nrm(ks[16], (D_MODEL,), 0.01),
    }

def second_block(x, c, norm_g, w_ada, b_ada, w_in, w_fft, na_rel_bias, ret_logit_fwd, ret_logit_bwd,
              conv_w, conv_b, conv_ln_g, conv_ln_b, conv_w_pw, w_out, final_g):
    c_act = jax.nn.silu(c)
    for l in range(DEPTH_2):
        mod = c_act @ w_ada[l] + b_ada[l]
        shift, scale, gate = jnp.split(mod, 3, axis=-1)
        h = _rmsnorm_2(x, norm_g[l]) * (1.0 + scale[:, None, :]) + shift[:, None, :]
        z = h @ w_in[l]
        (f_x, f_g, na_q, na_k, na_v, na_g, r_q, r_k, r_v, r_g,
         cv_a, cv_b, cv_g) = jnp.split(z, N_IN_PIECES, axis=-1)
        o_fft = _fourier_mix(f_x, w_fft[l]) * jax.nn.silu(f_g)
        o_na = _neighbourhood_attention(na_q, na_k, na_v, na_rel_bias[l]) * jax.nn.silu(na_g)
        o_ret = _retention(r_q, r_k, r_v, ret_logit_fwd[l], ret_logit_bwd[l]) * jax.nn.silu(r_g)
        o_cv = _conformer_conv(cv_a, cv_b, conv_w[l], conv_b[l], conv_ln_g[l], conv_ln_b[l],
                               conv_w_pw[l]) * jax.nn.silu(cv_g)
        y = jnp.concatenate([o_fft, o_na, o_ret, o_cv], axis=-1) @ w_out[l]
        x = x + gate[:, None, :] * y
    return _rmsnorm_2(x, final_g)


def setup_inputs(seed=0):
    out = dict(first_inputs(seed))
    for name, value in second_inputs(seed + 1).items():
        if name != "x":
            out[name + "_2"] = value
    return out


def reference(
    x, ffn1_norm, ffn1_w_gu, ffn1_w_down, mix_norm, w_in, qk_gain, sinks, cmp_pos, cmp_w1,
    cmp_w2, w_branch_a, w_branch_b, w_branch_c, w_out, ffn2_norm, ffn2_w_gu, ffn2_w_down, c_2,
    norm_g_2, w_ada_2, b_ada_2, w_in_2, w_fft_2, na_rel_bias_2, ret_logit_fwd_2,
    ret_logit_bwd_2, conv_w_2, conv_b_2, conv_ln_g_2, conv_ln_b_2, conv_w_pw_2, w_out_2,
    final_g_2,
):
    x = first_block(
        x, ffn1_norm, ffn1_w_gu, ffn1_w_down, mix_norm, w_in, qk_gain, sinks, cmp_pos, cmp_w1,
        cmp_w2, w_branch_a, w_branch_b, w_branch_c, w_out, ffn2_norm, ffn2_w_gu, ffn2_w_down,
    )
    return second_block(
        x, c_2, norm_g_2, w_ada_2, b_ada_2, w_in_2, w_fft_2, na_rel_bias_2, ret_logit_fwd_2,
        ret_logit_bwd_2, conv_w_2, conv_b_2, conv_ln_g_2, conv_ln_b_2, conv_w_pw_2, w_out_2,
        final_g_2,
    )


_drawn_inputs = setup_inputs


def setup_inputs(seed=0):
    import zlib

    import numpy as np

    out = dict(_drawn_inputs(seed))
    spreads = {}
    factors = {'qk_gain': 3.149,
     'sinks': 8.0,
     'cmp_pos': 8.0,
     'ffn2_norm': 2.83,
     'norm_g_2': 8.0,
     'b_ada_2': 7.006,
     'na_rel_bias_2': 8.0,
     'conv_b_2': 8.0,
     'conv_ln_g_2': 8.0,
     'conv_ln_b_2': 8.0,
     'final_g_2': 5.523}
    for name, (base, spread) in spreads.items():
        noise = np.random.default_rng([zlib.crc32(name.encode()), seed]).standard_normal(out[name].shape)
        drawn = base * np.exp(spread * noise) if base else spread * noise
        out[name] = __import__('jax').numpy.asarray(drawn.astype(out[name].dtype))
    for name, factor in factors.items():
        out[name] = (out[name] * factor).astype(out[name].dtype)
    return out
```

```python
from contextlib import ExitStack
from math import prod

import numpy as np
import concourse.bass as bass
from concourse import mybir

F32 = mybir.dt.float32
ALU = mybir.AluOpType
ACT = mybir.ActivationFunctionType
AXX = mybir.AxisListType.X

P = 128
S = 256
TT = S // P
D = 2048
DC = D // P
FF = 5632
FC = FF // P
DH = 64
EPS = 1e-6
W2 = 2 * P
HALF = 8
DOWN = 11
RING = 4
SLOT = DOWN * W2
NCMP, CMP_STRIDE, CMP_END = 15, 16, 31
TAPS = 31

GU_GROUPS, DOWN_GROUPS = FF // W2, D // W2
FFN_SLABS, FFN_GROUPS = 4 * GU_GROUPS + 4 * DOWN_GROUPS, GU_GROUPS + DOWN_GROUPS
PROJ, GATES, BRANCH, OUTG = 18, 24, 24, 8
MIX_SLABS = 2 * PROJ + 2 + 4 + 2 * GATES + 14 + 2 * OUTG
MIX_GROUPS = PROJ + 1 + GATES + BRANCH + OUTG
PIECE = 26
LAY_SLABS, LAY_GROUPS = 2 * PIECE + 2 + 2 * OUTG, PIECE + 4 + OUTG
S_F1, S_MIX = 0, FFN_SLABS
S_F2 = S_MIX + MIX_SLABS
S_LAY = [S_F2 + FFN_SLABS, S_F2 + FFN_SLABS + LAY_SLABS]
G_LOAD = 8
G_F1, G_MIX = G_LOAD, G_LOAD + FFN_GROUPS
G_F2 = G_MIX + MIX_GROUPS
G_LAY = [G_F2 + FFN_GROUPS, G_F2 + FFN_GROUPS + LAY_GROUPS]
G_END = G_LAY[1] + LAY_GROUPS
X_READY = [G_F1, G_MIX, G_F2, G_LAY[0], G_LAY[1], G_END]

NORMED = {0: (0, 2, 0), 1: (2, 2, 0), 2: (4, 2, 0), 3: (6, 2, 1), 4: (8, 2, 1), 5: (10, 2, 1),
          9: (12, 2, 2), 10: (14, 2, 2), 11: (16, 1, 3), 12: (17, 2, 4), 13: (19, 2, 4), 14: (21, 2, 4),
          16: (23, 1, 5), 17: (24, 1, 5)}
VALUES = {6: (0, 2), 7: (2, 2), 8: (4, 2), 11: (6, 1), 16: (7, 1), 17: (8, 1)}
CMP_GROUP = 15
A_COLS, B_Q, C_Q, C_KV = 2304, 2304, 3072, 3840
CGATE0, GATE0 = 4608, 4644
NEG = 1e33


def slopes(n):
    return [float(v) for v in np.float32(2.0) ** (np.float32(-8.0) * np.arange(1, n + 1, dtype=np.float32) / np.float32(n))]


SL_A, SL_B, SL_C = slopes(12), slopes(8), slopes(12)

CONST, _at = {}, 0
for _name, _w in (("ident", P), ("ones", P), ("blocks", P), ("eps", 1),
                  ("dist", 5 * 384), ("cdist", 2 * NCMP), ("cmask", 2 * NCMP),
                  ("cos", S), ("sin", S), ("rot", P), ("dpos", 2 * S), ("dneg", 2 * S),
                  ("dft", 2 * P), ("dcos", 2 * S), ("dsin", 2 * S), ("strip", 191), ("wmask", DH)):
    CONST[_name] = (_at, _at + _w)
    _at += _w
CONST_COLS = _at
PIECES = (2, 3, 4, 10, 11, 6, 7, 8, 0, 1, 5, 9, 12)
BASE_END, MIX_END = CONST["eps"][1], CONST["cmask"][1]


def constant_table():
    c = np.zeros((P, CONST_COLS), np.float32)

    def put(name, value):
        a, b = CONST[name]
        c[:value.shape[0], a:b] = value

    p = np.arange(P)
    put("ident", np.eye(P))
    put("ones", np.ones((P, P)))
    put("blocks", (p[:, None] // DH == p[None, :] // DH).astype(float))
    put("eps", np.full((P, 1), EPS))
    t = np.arange(S)
    d = t[:, None] - t[None, :]

    def tiles(keep, dist=d):
        m = np.where(keep, dist, NEG)
        return np.concatenate([m[:P, :P], m[P:, :]], axis=1)

    put("dist", np.concatenate([tiles((d >= 0) & (d <= 128)), tiles((d >= 0) & (d % 4 == 0)),
                                tiles((d >= 0) & (d % 16 == 0)), tiles((d >= 0) & (d <= 127)),
                                tiles(d >= 0)], axis=1))
    dc = t[:, None] - (CMP_STRIDE * np.arange(NCMP) + CMP_END)[None, :]
    put("cdist", np.concatenate([np.where(dc >= 0, dc, NEG)[:P], np.where(dc >= 0, dc, NEG)[P:]], 1))
    put("cmask", np.concatenate([(dc >= 0)[:P], (dc >= 0)[P:]], 1).astype(float))
    half = DH // 2
    inv = np.float32(10000.0) ** (-np.arange(half, dtype=np.float32) / np.float32(half))
    ang = (t.astype(np.float32)[:, None] * inv[None, :]).astype(np.float64)
    put("cos", np.cos(ang).T[p % half])
    put("sin", np.sin(ang).T[p % half])
    rot = np.zeros((P, P))
    for m in range(P):
        first = m % DH < half
        rot[m + half if first else m - half, m] = -1.0 if first else 1.0
    put("rot", rot)
    dts = (t[None, :] - t[:, None]).astype(float)
    put("dpos", np.concatenate([np.maximum(dts, 0)[:P], np.maximum(dts, 0)[P:]], 1))
    put("dneg", np.concatenate([np.maximum(-dts, 0)[:P], np.maximum(-dts, 0)[P:]], 1))
    a = 2 * np.pi * np.outer(p, p) / P
    put("dft", np.concatenate([np.cos(a), np.sin(a)], 1))
    a = 2 * np.pi * (np.outer(t, t) % S) / S
    n = 1 / np.sqrt(S * P)
    put("dcos", np.concatenate([n * np.cos(a)[:P], n * np.cos(a)[P:]], 1))
    put("dsin", np.concatenate([-n * np.sin(a)[:P], -n * np.sin(a)[P:]], 1))
    strip = np.zeros((62, 191))
    for r in range(2):
        for j in range(31):
            strip[31 * r + j, 78 - j + DH * r] = 1.0
    put("strip", strip)
    col = p % DH
    start = np.clip(col - 8, 0, DH - 16)
    kc = np.arange(DH)
    put("wmask", np.where((kc[None] >= start[:, None]) & (kc[None] < start[:, None] + 16), 0.0, -1e30))
    return c


PARAM_TILES = [
    [("ffn1_norm", 16), ("mix_norm", 16), ("ffn2_norm", 16), ("cmp_pos", 32), ("qk_gain", 6)],
    [("norm_g_2", 32), ("b_ada_2", 96)],
    [("conv_w_2a", 124)], [("conv_w_2b", 124)],
    [("conv_b_2", 8), ("conv_ln_g_2", 8), ("conv_ln_b_2", 8), ("final_g_2", 16), ("c_2", 16)],
]
PCOL, _at = {}, 0
for _tile in PARAM_TILES:
    for _name, _w in _tile:
        PCOL[_name] = _at
        _at += _w
PARAMS = _at

ADA_RING = FC * S
SILU = ADA_RING + 2 * DC * W2
ADA_ACC = SILU + 2 * 512
QK, VN = 0, 25 * S
GT = VN + TT * 9 * P
SQ, LN, RS, VRAW = GT, GT + 1024, GT + 2048, GT + 3072
CRAW, CBLK, CHID = GT + 4096, GT + 4608, GT + 5568
CTMP = CHID + 4 * 2 * NCMP
OT = GT + 48 * S
EB = OT + 12 * S
PT = EB + 2 * 1280
DIST = PT + 9 * P
UN = DIST + (CONST_COLS - MIX_END) + 96
RB = DIST + (CONST_COLS - MIX_END)
LQ, LV = 0, 16 * S
FX = LV + 2 * TT * 4 * P
LG = FX + 4 * S
CT = LG + 16 * S
UPAD = CT + 16 * S
UW = S + TAPS - 1
CY = UPAD + 4 * UW
NB = CY + 4 * S
LSQ = NB + 48 * DH
LT1, LT2 = LSQ + 1024, LSQ + 2048
assert LT2 + 1024 <= EB


class Signal:

    def __init__(self, handle, marks, final):
        self.handle, self.marks, self.final, self.n = handle, marks, final, 0

    def mark(self, *key):
        key = key[0] if len(key) == 1 else key
        self.n += 1
        self.marks[key] = self.n
        return self.handle, 1

    def after(self, *key):
        key = key[0] if len(key) == 1 else key
        return self.handle, self.marks[key] if self.final else 1


def build(nc, a, out, const, marks, final):
    ctx = ExitStack()
    with ctx:
        def sb(name, shape):
            return ctx.enter_context(nc.sbuf_tensor(name, shape, F32))

        def sem(name):
            return ctx.enter_context(nc.semaphore(name))

        def signal(name):
            return Signal(sem(name), marks.setdefault(name, {}), final)

        x = sb("x_res", [P, DC, S])
        h = sb("h", [P, DC, S])
        ring = sb("ring", [P, RING, SLOT])
        U = sb("U", [P, UN])
        base = sb("base_consts", [P, BASE_END])
        par = sb("params", [P, PARAMS])
        mod = sb("mod", [P, 2, 48])
        ascale = sb("ascale", [P, 2, DC])
        rstd = sb("rstd", [P, S])
        lnx = sb("lnx", [P, S])
        cact = sb("cact", [P, DC])
        sinks = sb("sinks_b", [P, 8])
        logit = sb("logit_b", [P, 4, 8])
        lgt = sb("lg_tmp", [P, 3, 32])
        w2 = sb("cmp_w2_sb", [P, 2, 2, DH])
        negmax = sb("negmax", [P, 2, 6])
        den = sb("den", [P, 2, 6])
        rden = sb("rden", [P, 2, 6])
        gn = sb("gn", [P, TT, 36])
        kc = sb("kc", [P, NCMP])
        vc = sb("vc", [P, 2, DH])
        kcs = sb("kcs", [P, 3, NCMP])
        ps = ctx.enter_context(nc.psum_tensor("ps", [P, 8, 512], F32))

        def u(start, *shape):
            v = U[0:shape[0], start:start + prod(shape[1:])]
            if len(shape) == 3:
                v = v.rearrange("p (a b) -> p a b", a=shape[1])
            if len(shape) == 4:
                v = v.rearrange("p (a b c) -> p a b c", a=shape[1], b=shape[2])
            return v

        def cst(name, rows=P):
            lo, hi = CONST[name]
            if hi <= BASE_END:
                return base[0:rows, lo:hi]
            at = DIST + lo - (BASE_END if hi <= MIX_END else MIX_END)
            return U[0:rows, at:at + hi - lo]

        def pcol(name, j=0, n=1):
            return par[:, PCOL[name] + j:PCOL[name] + j + n]

        ident, ones, blocks, eps = cst("ident"), cst("ones"), cst("blocks"), cst("eps")
        aT = u(0, P, FC, S)
        merged = u(GT, P, 48, S)
        qk, vn = u(QK, P, 25, S), u(VN, P, TT, 9, P)
        oT = u(OT, P, 12, S)
        ebuf, pT = u(EB, P, 2, 1280), u(PT, P, 9 * P)
        lq, lv = u(LQ, P, 16, S), u(LV, P, 2 * TT, 4, P)
        lgate, cT, cy = u(LG, P, 16, S), u(CT, P, 16, S), u(CY, P, 4, S)
        upad, fx = u(UPAD, P, 4, UW), u(FX, P, 4, S)
        nbias = u(NB, P, 8, 6, DH)

        const_in, par_in, x_in, late_in, small_in, out_done = (sem(n) for n in (
            "const_in", "par_in", "x_in", "late_in", "small_in", "out_done"))
        slab_in = [sem(f"slab_in{k}") for k in range(RING)]
        ada_in = [sem(f"ada_in{k}") for k in range(2)]
        slab_done = sem("slab_done")
        evacuated = sem("evacuated")
        silu_done = sem("silu_done")
        ada_step, ada_sum, ada_red = sem("ada_step"), sem("ada_sum"), sem("ada_red")
        h_ready, sq_ready, sumsq, rstd_ready = (signal(n) for n in ("h_ready", "sq_ready", "sumsq", "rstd_ready"))
        xt, pt_done, par_ready = signal("x_transposed"), signal("params_transposed"), signal("params_ready")
        gp_done = signal("gpsimd_done")
        pe_out = signal("small_products")
        act_out = signal("act_results")
        vec_out = signal("vector_results")
        part_done = signal("branch_part")
        scores, biased, expd, probs = (signal(n) for n in ("scores", "biased", "exponentials", "probs"))
        ptr, ptc, pv, o_out = (signal(n) for n in ("probs_transposed", "probs_copied", "values_summed", "heads_out"))

        slabs = []

        def rows(w, chunk0, n):
            return w.rearrange("(c p) n -> p c n", p=P)[:, chunk0:chunk0 + n, :]

        def slot_view(n, chunks, cols):
            return ring[:, n % RING, 0:chunks * cols].rearrange("p (c w) -> p c w", c=chunks)

        def halves(w, col, cols=W2):
            for k in range(2):
                n = len(slabs)
                slabs.append([(slot_view(n, HALF, cols), rows(w, k * HALF, HALF)[:, :, col:col + cols])])

        def paired_heads(w, col, per, j0):
            for k in range(2):
                n = len(slabs)
                view = slot_view(n, HALF, W2)
                src = rows(w, k * HALF, HALF)[:, :, col:col + 2 * per * DH].rearrange("p c (g j d) -> p c g j d", g=2, j=per)
                slabs.append([(view[:, :, (2 * j + g) * DH:(2 * j + g + 1) * DH], src[:, :, g, j0 + j, :])
                              for j in range(2) for g in range(2)])

        def stream():
            for j in range(GU_GROUPS):
                halves(a["ffn1_w_gu"][0], j * W2)
                halves(a["ffn1_w_gu"][0], FF + j * W2)
            down_slabs(a["ffn1_w_down"][0])
            w_in = a["w_in"][0]
            for p in range(PROJ):
                if p in (9, 10):
                    paired_heads(w_in, B_Q, 4, 2 * (p - 9))
                elif p in (12, 13, 14):
                    paired_heads(w_in, C_Q, 6, 2 * (p - 12))
                else:
                    halves(w_in, p * W2)
            halves(w_in, CGATE0, 36)
            for kv in range(2):
                halves(a["cmp_w1"][0, kv], 0)
            for p in range(GATES):
                halves(w_in, GATE0 + p * W2)
            for k in range(2):
                n = len(slabs)
                slabs.append([(slot_view(n, 2, 1024), rows(a["w_branch_a"][0], 0, 2)[:, :, k * 1024:(k + 1) * 1024])])
            for w, per, cols in ((a["w_branch_b"][0], 4, 512), (a["w_branch_c"][0], 6, 256)):
                src = w.rearrange("(g j d) n -> g d j n", g=2, j=per)
                for k in range(D // cols):
                    n = len(slabs)
                    v = slot_view(n, per, cols)
                    slabs.append([(v[g * DH:(g + 1) * DH], src[g][:, :, k * cols:(k + 1) * cols]) for g in range(2)])
            for p in range(OUTG):
                halves(a["w_out"][0], p * W2)
            for j in range(GU_GROUPS):
                halves(a["ffn2_w_gu"][0], j * W2)
                halves(a["ffn2_w_gu"][0], FF + j * W2)
            down_slabs(a["ffn2_w_down"][0])
            for l in range(2):
                for piece in PIECES:
                    for k in range(2):
                        halves(a["w_in_2"][l], piece * 512 + k * W2)
                for w in (a["w_fft_2"][l], a["conv_w_pw_2"][l]):
                    n = len(slabs)
                    slabs.append([(slot_view(n, 4, 512), rows(w, 0, 4))])
                for p in range(OUTG):
                    halves(a["w_out_2"][l], p * W2)

        def down_slabs(w):
            for g in range(DOWN_GROUPS):
                for k in range(4):
                    n = len(slabs)
                    slabs.append([(slot_view(n, DOWN, W2), rows(w, k * DOWN, DOWN)[:, :, g * W2:(g + 1) * W2])])

        stream()
        assert len(slabs) == S_LAY[1] + LAY_SLABS
        loaded, _count = [], [0] * RING
        for n, parts in enumerate(slabs):
            _count[n % RING] += 16 * len(parts)
            loaded.append(_count[n % RING])

        def slab_loaded(n, more=0):
            return slab_in[n % RING], loaded[n] + more

        def acc(g, side=0):
            return ps[:, 2 * (g % 2) + side, :]

        def pt_bank(i):
            return ps[:, 1 if i < 4 else 7, (i % 4) * P:(i % 4 + 1) * P] if i < 8 else ps[:, 3, S:S + P]

        dist = cst("dist").rearrange("p (t c) -> p t c", t=5)

        def dist_of(table, T):
            return dist[:, table, 0:P] if T == 0 else dist[:, table, P:P + S]

        def segment(T, bank, col, n, q, k, half, **more):
            return dict(T=T, bank=bank, col=col, n=n, q=q, k=k, half=half, **more)

        def block_of(T, col, n, val):
            return dict(T=T, col=col, n=n, v=val)

        def finish(units, name):
            for i, un in enumerate(units):
                un["key"] = (*name, i)
                un["prev"] = units[i - 1]["key"] if i else None
                un["prev2"] = units[i - 2]["key"] if i > 1 else None
                un["e"] = i % 2
                for T in range(TT):
                    mine = [b for b in un["blocks"] if b["T"] == T]
                    for b in mine:
                        b["first"], b["last"] = b is mine[0], b is mine[-1]
            return units

        def units_mix():
            units = []
            for hh in range(4):
                half, c = hh % 2, [(4 * g + hh) // 2 for g in range(3)]
                vcols = slice(half * DH, half * DH + DH)
                segs = [segment(0, 4, g * P, P, qk[:, c[g], :], qk[:, 6 + c[g], :], half, dist=dist_of(g, 0), slope=SL_A[4 * g + hh])
                        for g in range(3)]
                segs += [segment(1, 5 + g // 2, (g % 2) * S, S, qk[:, c[g], :], qk[:, 6 + c[g], :], half, dist=dist_of(g, 1),
                                 slope=SL_A[4 * g + hh]) for g in range(3)]
                blks = [block_of(0, g * P, P, vn[:, 0, c[g], vcols]) for g in range(3)]
                blks += [block_of(1, 512 + g * S + kb * P, P, vn[:, kb, c[g], vcols]) for g in range(3) for kb in range(TT)]
                units.append(dict(segs=segs, blocks=blks, half=half, out=oT[:, hh // 2, :],
                                  softmax=[dict(col=0, n=384), dict(col=512, n=768)]))
            for hh in range(8):
                j, g = hh % 4, hh // 4
                vcols = slice(g * DH, g * DH + DH)
                segs = [segment(T, 4 + T, 0, (T + 1) * P, qk[:, 12 + j, :], qk[:, 16, :], g, dist=dist_of(3, T), slope=SL_B[hh])
                        for T in range(TT)]
                blks = [block_of(T, 512 * T + kb * P, P, vn[:, kb, 6, vcols]) for T in range(TT) for kb in range(T + 1)]
                units.append(dict(segs=segs, blocks=blks, half=g, out=oT[:, 2 + j, :], sink=hh,
                                  softmax=[dict(col=0, n=P + 1), dict(col=512, n=S + 1)]))
            for hh in range(12):
                j, g = hh % 6, hh // 6
                vcols = slice(g * DH, g * DH + DH)
                q = qk[:, 17 + j, :]
                segs, soft, blks, cmps = [], [], [], []
                for T in range(TT):
                    n, e0 = (T + 1) * P, 512 * T
                    cb, cc = (4, S) if T == 0 else (6, 0)
                    ce = (cb - 4) * 512 + cc
                    for i in range(2):
                        segs.append(segment(T, 4 + T, i * n, n, q, qk[:, 23 + i, :], g, dist=dist_of(4, T), slope=SL_C[hh]))
                    segs.append(segment(T, cb, cc, NCMP, q, kc[:, :], g, dist=cst("cdist")[:, T * NCMP:(T + 1) * NCMP], slope=SL_C[hh]))
                    soft += [dict(col=ce, n=NCMP, mask=cst("cmask")[:, T * NCMP:(T + 1) * NCMP]), dict(col=e0, n=n), dict(col=e0 + n, n=n)]
                    blks += [block_of(T, e0 + i * n + kb * P, P, vn[:, kb, 7 + i, vcols]) for i in range(2) for kb in range(T + 1)]
                    cmps.append(block_of(T, ce, NCMP, vc[0:NCMP, g, :]))
                units.append(dict(segs=segs, blocks=blks + cmps, half=g, out=oT[:, 6 + j, :], gate=hh, softmax=soft))
            return finish(units, ("mix",))

        def units_na(l):
            units = []
            for hh in range(8):
                half, c = hh % 2, hh // 2
                vcols = slice(half * DH, half * DH + DH)
                segs = [segment(T, 4 + T, 0, S, lq[:, c, :], lq[:, 4 + c, :], half,
                                nbias=nbias[:, hh, 2 - 2 * T:6 - 2 * T, :].rearrange("p a b -> p (a b)")) for T in range(TT)]
                blks = [block_of(T, 512 * T + kb * P, P, lv[:, kb, c, vcols]) for T in range(TT) for kb in range(TT)]
                units.append(dict(segs=segs, blocks=blks, half=half, out=cT[:, 4 + c, :],
                                  softmax=[dict(col=0, n=S), dict(col=512, n=S)]))
            return finish(units, ("na", l))

        def units_ret(l):
            units = []
            for hh in range(8):
                half, c = hh % 2, hh // 2
                vcols = slice(half * DH, half * DH + DH)
                segs = [segment(st, 4 + st, 0, S, lq[:, 12 + c, :], lq[:, 8 + c, :], half) for st in range(TT)]
                units.append(dict(segs=segs, blocks=[], half=half, head=hh, out=cT[:, 8 + c, :],
                                  v=[lv[:, TT + st, c, vcols] for st in range(TT)],
                                  before=("ret", l, hh - 1) if hh else ("na", l, 7)))
            return finish(units, ("ret", l))

        rowbuf = u(4096, P, 5, P)

        def param_rows(t, r0, src):
            n, w = src.shape
            return rowbuf[r0:r0 + n, t, 0:w], src

        by_rows = lambda ap: ap.rearrange("(r c) -> r c", c=P)
        PAR_LOADS = [param_rows(0, 0, by_rows(a["ffn1_norm"][0])), param_rows(0, 16, by_rows(a["mix_norm"][0])),
                     param_rows(0, 32, by_rows(a["ffn2_norm"][0]))]
        PAR_LOADS += [param_rows(0, 48 + 16 * kv, a["cmp_pos"][0, kv].rearrange("(c e) d -> c (e d)", e=2)) for kv in range(2)]
        gains = a["qk_gain"][0].rearrange("a b d -> (a b) d")
        PAR_LOADS += [(rowbuf[80:86, 0, k * DH:(k + 1) * DH], gains) for k in range(2)]
        PAR_LOADS += [param_rows(1, 16 * l, by_rows(a["norm_g_2"][l])) for l in range(2)]
        PAR_LOADS += [param_rows(1, 32 + 48 * l, by_rows(a["b_ada_2"][l])) for l in range(2)]
        PAR_LOADS += [param_rows(2 + l, 0, a["conv_w_2"][l].rearrange("t (c p) -> (t c) p", p=P)) for l in range(2)]
        for k, name in enumerate(("conv_b_2", "conv_ln_g_2", "conv_ln_b_2")):
            PAR_LOADS += [param_rows(4, 8 * k + 4 * l, by_rows(a[name][l])) for l in range(2)]
        PAR_LOADS += [param_rows(4, 24, by_rows(a["final_g_2"])), param_rows(4, 40, by_rows(a["c_2"][0]))]
        N_PAR = len(PAR_LOADS)
        SMALL, LATE = 16 * 7, 16 * 33

        block = ctx.enter_context(nc.Block())

        @block.sync
        def _(sp):
            for T in range(TT):
                sp.dma_start(u(0, P, TT, D)[:, T, :], a["x"][0, T * P:(T + 1) * P, :]).then_inc(x_in, 16)

            def load(n):
                if n >= RING:
                    sp.wait_ge(slab_done, n - RING + 1)
                for dst, src in slabs[n]:
                    sp.dma_start(dst, src).then_inc(slab_in[n % RING], 16)

            def load_ffn(w_gu, w_down, s0):
                for n in range(s0, s0 + 8):
                    load(n)
                with sp.Fori(1, GU_GROUPS // 2) as i:
                    for k in range(8):
                        n = s0 + k
                        col = (k // 4) * W2 + (FF if k % 4 >= 2 else 0)
                        at = sp.snap(i * (2 * W2) + col)
                        sp.wait_ge(slab_done, i * 8 + (n - RING + 1))
                        sp.dma_start(slot_view(n, HALF, W2),
                                     rows(w_gu, (k % 2) * HALF, HALF)[:, :, bass.ds(at, W2)]).then_inc(slab_in[n % RING], 16)
                s1 = s0 + 4 * GU_GROUPS
                with sp.Fori(0, DOWN_GROUPS // 2) as i:
                    for k in range(8):
                        n = s1 + k
                        at = sp.snap(i * (2 * W2) + (k // 4) * W2)
                        sp.wait_ge(slab_done, i * 8 + (n - RING + 1))
                        sp.dma_start(slot_view(n, DOWN, W2),
                                     rows(w_down, (k % 4) * DOWN, DOWN)[:, :, bass.ds(at, W2)]).then_inc(slab_in[n % RING], 16)

            load_ffn(a["ffn1_w_gu"][0], a["ffn1_w_down"][0], S_F1)
            for n in range(S_MIX, S_F2):
                load(n)
            load_ffn(a["ffn2_w_gu"][0], a["ffn2_w_down"][0], S_F2)
            for n in range(S_LAY[0], S_LAY[1] + LAY_SLABS):
                load(n)
            for T in range(TT):
                sp.wait_ge(*vec_out.after("res", 4 * T + 3))
                sp.dma_start(out[0, T * P:(T + 1) * P, :], u(0, P, TT, D)[:, T, :]).then_inc(out_done, 16)
            sp.wait_ge(out_done, 32)

        @block.gpsimd
        def _(pool):
            for l in range(2):
                w = a["w_ada_2"][l].rearrange("(c p) n -> p c n", p=P)
                slot = [u(ADA_RING + k * DC * W2, P, DC, W2) for k in range(2)]
                if l == 1:
                    pool.wait_ge(evacuated, G_F2)
                    pool.dma_start(U[:, DIST:DIST + CONST_COLS - MIX_END], const[:, MIX_END:CONST_COLS]).then_inc(late_in, 16)
                    for ll in range(2):
                        for r in range(2):
                            src = a["na_rel_bias_2"][ll, :, 5 - r:11 - r, :].rearrange("h d j -> j h d")
                            dst = u(RB, P, 2, 8, 6)[31 * r:31 * r + 31, ll]
                            for hh in range(8):
                                pool.dma_start(dst[:, hh, :], src[:, hh, :], allow_slow_non_contiguous=True).then_inc(late_in, 16)
                for k in range(2):
                    pool.dma_start(slot[k], w[:, :, k * W2:(k + 1) * W2]).then_inc(ada_in[k], 16)
                with pool.Fori(0, 11) as i:
                    for k in range(2):
                        pool.wait_ge(ada_sum, i * 2 + (24 * l + 1 + k))
                        pool.dma_start(slot[k], w[:, :, bass.ds(i * (2 * W2) + (k + 2) * W2, W2)]).then_inc(ada_in[k], 16)

        @block.tensor
        def _(pe):
            mm = nc.tensor.matmul

            def transpose(dst, src):
                n = src.shape[0]
                return nc.tensor.transpose(dst, src, ident[0:n, 0:n])

            def halves_product(g, n, moving, cols=W2):
                pe.wait_ge(evacuated, g - 1)
                bank = acc(g)
                for c in range((cols + P - 1) // P):
                    w = min(P, cols - c * P)
                    for kk in range(DC):
                        if c == 0 and kk % HALF == 0:
                            pe.wait_ge(*slab_loaded(n + kk // HALF))
                        last = mm(bank[0:w, c * S:(c + 1) * S], slot_view(n + kk // HALF, HALF, cols)[:, kk % HALF, c * P:c * P + w],
                                  moving[:, kk, :], start=kk == 0, stop=kk == DC - 1)
                        if kk % HALF == HALF - 1 and c == (cols - 1) // P:
                            last.then_inc(slab_done, 1)

            def norm_sum(r):
                for c in range(DC):
                    if c % HALF == 0:
                        pe.wait_ge(*sq_ready.after(r, c // HALF))
                    last = mm(ps[:, 5, 0:S], ones, u(0, P, DC, S)[:, c, :], start=c == 0, stop=c == DC - 1)
                last.then_inc(*sumsq.mark(r))

            def ffn(f, s0, g0, r):
                norm_sum(r)
                pe.wait_ge(*h_ready.after(r))
                with pe.Fori(0, GU_GROUPS // 2) as i:
                    for k in range(2):
                        pe.wait_ge(evacuated, i * 2 + (g0 + k - 1))
                        for side in range(2):
                            n = s0 + 4 * k + 2 * side
                            for c in range(2):
                                for kk in range(DC):
                                    m = n + kk // HALF
                                    if c == 0 and kk % HALF == 0:
                                        pe.wait_ge(slab_in[m % RING], i * 32 + loaded[m])
                                    last = mm(acc(g0 + k, side)[:, c * S:(c + 1) * S],
                                              slot_view(m, HALF, W2)[:, kk % HALF, c * P:(c + 1) * P],
                                              h[:, kk, :], start=kk == 0, stop=kk == DC - 1)
                                    if c == 1 and kk % HALF == HALF - 1:
                                        last.then_inc(slab_done, 1)
                s1, g1 = s0 + 4 * GU_GROUPS, g0 + GU_GROUPS
                pe.wait_ge(evacuated, g1)
                with pe.Fori(0, DOWN_GROUPS // 2) as i:
                    for k in range(2):
                        pe.wait_ge(evacuated, i * 2 + (g1 + k - 1))
                        for q in range(4):
                            m = s1 + 4 * k + q
                            pe.wait_ge(slab_in[m % RING], i * 32 + loaded[m])
                            for c in range(2):
                                for kk in range(DOWN):
                                    last = mm(acc(g1 + k, c)[:, 0:S], slot_view(m, DOWN, W2)[:, kk, c * P:(c + 1) * P],
                                              aT[:, q * DOWN + kk, :], start=q == 0 and kk == 0,
                                              stop=q == 3 and kk == DOWN - 1)
                            last.then_inc(slab_done, 1)
                        pe.wait_ge(ada_sum, i * 6 + (24 * f + 3 * k + 3))
                        for b in range(3):
                            for c in range(2):
                                last = mm(ps[:, 4, bass.ds(i * 12 + (6 * k + 2 * b + c), 1)],
                                          u(ADA_ACC, P, 6, W2)[:, 3 * k + b, c * P:(c + 1) * P], ones[:, 0:1],
                                          start=True, stop=True)
                        last.then_inc(ada_red, 1)

            pe.wait_ge(const_in, 32)
            pe.wait_ge(par_in, 16 * N_PAR)
            for t, tile in enumerate(PARAM_TILES):
                n = sum(w for _, w in tile)
                transpose(ps[:, 4 + t // 4, (t % 4) * P:(t % 4) * P + n], u(4096, P, 5, P)[0:n, t, :]).then_inc(*pt_done.mark(t))
            pe.wait_ge(x_in, 32)
            for g in range(G_LOAD):
                if g >= 2:
                    pe.wait_ge(evacuated, g - 1)
                for c in range(2):
                    for T in range(TT):
                        at = (2 * g + c) * P
                        last = transpose(acc(g)[:, c * S + T * P:c * S + (T + 1) * P], u(0, P, TT, D)[:, T, at:at + P])
                last.then_inc(*xt.mark(g))

            ffn(0, S_F1, G_F1, 0)

            norm_sum(1)
            pe.wait_ge(*h_ready.after(1))

            def proj_lag(p):
                if p in NORMED:
                    n = NORMED[p][1]
                    pe.wait_ge(*act_out.after("psq", p))
                    if p > 0:
                        pe.wait_ge(*act_out.after("pln", max(q for q in NORMED if q < p)))
                    mm(ps[:, 5, 0:n * S], blocks, u(SQ + (p % 2) * 512, P, n * S), start=True, stop=True).then_inc(*pe_out.mark("pstat", p))
                if p in VALUES:
                    n = VALUES[p][1]
                    pe.wait_ge(evacuated, G_MIX + p + 1)
                    prev = max([q for q in VALUES if q < p], default=None)
                    if prev is not None:
                        pe.wait_ge(*act_out.after("vn", prev))
                    for c in range(n):
                        for T in range(TT):
                            last = transpose(ps[:, 7, (c * TT + T) * P:(c * TT + T + 1) * P],
                                             u(VRAW + (p % 2) * 512, P, 2, S)[:, c, T * P:(T + 1) * P])
                    last.then_inc(*pe_out.mark("vt", p))

            for p in range(PROJ):
                halves_product(G_MIX + p, S_MIX + 2 * p, h)
                if p > 0:
                    proj_lag(p - 1)
            sg, gg = S_MIX + 2 * PROJ, G_MIX + PROJ
            halves_product(gg, sg, h, 36)
            proj_lag(PROJ - 1)

            pe.wait_ge(*vec_out.after("cblk"))
            for kv in range(2):
                n = sg + 2 + 2 * kv
                for hc in range(2):
                    for c in range(DC):
                        if hc == 0 and c % HALF == 0:
                            pe.wait_ge(*slab_loaded(n + c // HALF))
                        last = mm(ps[:, 4, (2 * kv + hc) * 30:(2 * kv + hc) * 30 + 30],
                                  slot_view(n + c // HALF, HALF, W2)[:, c % HALF, hc * P:(hc + 1) * P],
                                  u(CBLK + kv * 480, P, DC, 30)[:, c, :], start=c == 0, stop=c == DC - 1)
                        if hc == 1 and c % HALF == HALF - 1:
                            last.then_inc(slab_done, 1)
            pe.wait_ge(*vec_out.after("cgate"))
            for T in range(TT):
                last = transpose(ps[:, 7, T * 36:T * 36 + 36], u(CTMP, 36, S)[:, T * P:(T + 1) * P])
            last.then_inc(*pe_out.mark("gn"))
            pe.wait_ge(*act_out.after("chid"))
            pe.wait_ge(small_in, SMALL)
            hid = u(CHID, P, 4, 2, NCMP)
            for g in range(2):
                for hc in range(2):
                    mm(ps[g * DH:(g + 1) * DH, 6, 64:64 + NCMP], w2[:, 0, hc, :], hid[:, hc, g, :], start=hc == 0, stop=hc == 1)
            for g in range(2):
                for hc in range(2):
                    last = mm(ps[0:NCMP, 6, 128 + g * DH:128 + (g + 1) * DH], hid[:, 2 + hc, g, :], w2[:, 1, hc, :],
                              start=hc == 0, stop=hc == 1)
            last.then_inc(*pe_out.mark("kcvc"))
            pe.wait_ge(*act_out.after("kcsq"))
            mm(ps[:, 5, 0:NCMP], blocks, kcs[:, 0, :], start=True, stop=True).then_inc(*pe_out.mark("kcstat"))

            def scores_of(un):
                key, segs = un["key"], un["segs"]
                if un["prev"] is not None:
                    pe.wait_ge(*biased.after(un["prev"]))
                for seg in segs:
                    rows_ = slice(seg["half"] * DH, seg["half"] * DH + DH)
                    last = mm(ps[:, seg["bank"], seg["col"]:seg["col"] + seg["n"]],
                              seg["q"][rows_, seg["T"] * P:(seg["T"] + 1) * P], seg["k"][rows_, 0:seg["n"]],
                              start=True, stop=True)
                last.then_inc(*scores.mark(key))

            def transposes_of(un):
                pe.wait_ge(*probs.after(un["key"]))
                if un["prev"] is not None:
                    pe.wait_ge(*ptc.after(un["prev"]))
                    pe.wait_ge(*o_out.after(un["prev"]))
                for i, b in enumerate(un["blocks"]):
                    last = transpose(pt_bank(i)[0:b["n"], :], ebuf[:, un["e"], b["col"]:b["col"] + b["n"]])
                last.then_inc(*ptr.mark(un["key"]))

            def values_of(un):
                pe.wait_ge(*ptc.after(un["key"]))
                for i, b in sorted(enumerate(un["blocks"]), key=lambda ib: ib[1]["T"]):
                    last = mm(ps[un["half"] * DH:(un["half"] + 1) * DH, 3, b["T"] * P:(b["T"] + 1) * P],
                              b["v"], pT[0:b["n"], i * P:(i + 1) * P], start=b["first"], stop=b["last"])
                last.then_inc(*pv.mark(un["key"]))

            def decayed_values(un):
                pe.wait_ge(*biased.after(un["key"]))
                pe.wait_ge(*o_out.after(un["before"]))
                r0, hh = un["half"] * DH, un["head"]
                for st in range(TT):
                    last = mm(ps[r0:r0 + DH, 3, 0:S], un["v"][st], ebuf[:, hh % 2, st * S:(st + 1) * S],
                              start=st == 0, stop=st == TT - 1)
                last.then_inc(*pv.mark(un["key"]))

            first = units_mix()
            pe.wait_ge(*vec_out.after("qk", PROJ - 1))
            pe.wait_ge(*act_out.after("vn", PROJ - 1))
            pe.wait_ge(*vec_out.after("kc"))
            pe.wait_ge(*act_out.after("gn"))
            for step in range(len(first) + 1):
                if step < len(first):
                    scores_of(first[step])
                if step > 0:
                    transposes_of(first[step - 1])
                if step < GATES:
                    halves_product(gg + 1 + step, sg + 6 + 2 * step, h)
                if step > 0:
                    values_of(first[step - 1])

            g, n = gg + 1 + GATES, sg + 6 + 2 * GATES
            for o0, per, cols, count in ((0, 2, 1024, 2), (2, 4, 512, 4), (6, 6, 256, 8)):
                pe.wait_ge(*o_out.after(first[{0: 3, 2: 11, 6: 23}[o0]]["key"]))
                for _k in range(count):
                    pe.wait_ge(*slab_loaded(n))
                    for part in range(cols // W2):
                        pe.wait_ge(evacuated, g - 1)
                        for c in range(2):
                            for j in range(per):
                                at = part * W2 + c * P
                                last = mm(acc(g)[:, c * S:(c + 1) * S], slot_view(n, per, cols)[:, j, at:at + P],
                                          oT[:, o0 + j, :], start=j == 0, stop=j == per - 1)
                        if part == cols // W2 - 1:
                            last.then_inc(slab_done, 1)
                        else:
                            last.then_inc(*part_done.mark(g))
                        g += 1
                    n += 1
            pe.wait_ge(evacuated, g)
            for p in range(OUTG):
                halves_product(g + p, n + 2 * p, merged)

            ffn(1, S_F2, G_F2, 2)

            for l in range(2):
                s0, g0 = S_LAY[l], G_LAY[l]
                if l == 0:
                    pe.wait_ge(late_in, LATE)
                rbl = u(RB, P, 2, 48)[0:62, l, :]
                strip = cst("strip", 62)
                for b in range(8):
                    if b >= 2:
                        pe.wait_ge(*vec_out.after("nb", l, b - 2))
                    elif b == 0:
                        pe.wait_ge(evacuated, g0)
                    for k in range(8):
                        at = 63 - (8 * b + k)
                        last = mm(ps[:, 6 + b % 2, k * 48:(k + 1) * 48], strip[:, at:at + P],
                                  rbl, start=True, stop=True)
                    last.then_inc(*pe_out.mark("nb", l, b))
                norm_sum(3 + l)
                pe.wait_ge(*h_ready.after(3 + l))

                def lay_lag(p):
                    if p in (10, 11, 12, 13):
                        pe.wait_ge(evacuated, g0 + p + 1)
                        if p > 10:
                            pe.wait_ge(*vec_out.after("rotp", l, p - 1))
                        mm(ps[:, 6, :], cst("rot"), u(LQ + (8 + 2 * (p - 10)) * S, P, 512), start=True, stop=True
                           ).then_inc(*pe_out.mark("rot", l, p))
                    if p in (4, 5, 14, 15):
                        pe.wait_ge(evacuated, g0 + p + 1)
                        if p in (5, 15):
                            pe.wait_ge(*act_out.after("lv", l, p - 1))
                        if p == 14:
                            pe.wait_ge(*ptc.after("na", l, 7))
                        for c in range(2):
                            for T in range(TT):
                                last = transpose(ps[:, 7, (c * TT + T) * P:(c * TT + T + 1) * P],
                                                 u(LT1, P, 2, 2, S)[:, p % 2, c, T * P:(T + 1) * P])
                        last.then_inc(*pe_out.mark("lvt", l, p))

                na, ret = units_na(l), units_ret(l)
                for p in range(PIECE):
                    if 6 <= p < 14:
                        scores_of(na[p - 6])
                    if 6 < p <= 14:
                        transposes_of(na[p - 7])
                    if 18 <= p:
                        if p == 18:
                            pe.wait_ge(*vec_out.after("rotq", l, 13))
                            pe.wait_ge(*act_out.after("lv", l, 15))
                        scores_of(ret[p - 18])
                    halves_product(g0 + p, s0 + 2 * p, h)
                    if 6 < p <= 14:
                        if p == 7:
                            pe.wait_ge(*act_out.after("lv", l, 5))
                        values_of(na[p - 7])
                    if p > 0:
                        lay_lag(p - 1)
                    if 18 < p:
                        decayed_values(ret[p - 19])
                decayed_values(ret[7])

                for c in range(4):
                    if c > 0:
                        pe.wait_ge(*vec_out.after("fp", l, c - 1))
                    else:
                        pe.wait_ge(*biased.after("ret", l, 7))
                    for T in range(TT):
                        last = mm(ps[:, 6, T * S:(T + 1) * S], fx[:, c, T * P:(T + 1) * P], cst("dft"), start=True, stop=True)
                    last.then_inc(*pe_out.mark("fp", l, c))
                    pe.wait_ge(*vec_out.after("fp", l, c))
                    if c > 0:
                        pe.wait_ge(*act_out.after("fy", l, c - 1))
                    fp = u(LT1, P, TT, 2, P)
                    for i, (part, tab) in enumerate(((0, "dcos"), (1, "dsin"))):
                        for T in range(TT):
                            last = mm(ps[:, 7, 0:S], fp[:, T, part, :], cst(tab)[:, T * S:(T + 1) * S],
                                      start=i == 0 and T == 0, stop=i == 1 and T == 1)
                    last.then_inc(*pe_out.mark("fy", l, c))
                for c in range(2):
                    pe.wait_ge(*act_out.after("rsq", l, c))
                    mm(ps[:, 5, :], blocks, u(LSQ + 512 * c, P, 512), start=True, stop=True).then_inc(*pe_out.mark("rstat", l, c))
                    pe.wait_ge(*act_out.after("rrs", l, c))
                pe.wait_ge(*vec_out.after("tap", l, 3, TAPS - 1))
                for c in range(4):
                    last = mm(ps[:, 5, 0:S], ones, cy[:, c, :], start=c == 0, stop=c == 3)
                last.then_inc(*pe_out.mark("mean", l))
                pe.wait_ge(*act_out.after("ysq", l))
                for c in range(4):
                    last = mm(ps[:, 6, 0:S], ones, u(LSQ, P, 4, S)[:, c, :], start=c == 0, stop=c == 3)
                last.then_inc(*pe_out.mark("var", l))
                g, n = g0 + PIECE, s0 + 2 * PIECE
                for which, moving in ((0, fx), (1, cy)):
                    pe.wait_ge(*slab_loaded(n))
                    pe.wait_ge(*(act_out.after("fy", l, 3) if which == 0 else vec_out.after("csilu", l)))
                    for part in range(2):
                        pe.wait_ge(evacuated, g - 1)
                        for c in range(2):
                            for j in range(4):
                                at = part * W2 + c * P
                                last = mm(acc(g)[:, c * S:(c + 1) * S], slot_view(n, 4, 512)[:, j, at:at + P],
                                          moving[:, j, :], start=j == 0, stop=j == 3)
                        last.then_inc(*(part_done.mark(g) if part == 0 else (slab_done, 1)))
                        g += 1
                    n += 1
                pe.wait_ge(evacuated, g)
                pe.wait_ge(*vec_out.after("gated", l))
                for p in range(OUTG):
                    halves_product(g + p, n + 2 * p, cT)

            norm_sum(5)
            pe.wait_ge(*h_ready.after(5))
            for i in range(8):
                T, c4 = i // 4, i % 4
                if i >= 2:
                    pe.wait_ge(*vec_out.after("res", i - 2))
                for c in range(4):
                    last = transpose(ps[:, i % 2, c * P:(c + 1) * P], h[:, 4 * c4 + c, T * P:(T + 1) * P])
                last.then_inc(*pe_out.mark("res", i))

        @block.scalar
        def _(act):
            fn = nc.scalar.activation

            def chained(ins, *key):
                ins.then_inc(*act_out.mark(*key))
                act.wait_ge(*act_out.after(*key))

            act.dma_start(base[:, :], const[:, 0:BASE_END]).then_inc(const_in, 16)
            act.dma_start(U[:, DIST:DIST + MIX_END - BASE_END], const[:, BASE_END:MIX_END]).then_inc(const_in, 16)
            for dst, src in PAR_LOADS:
                act.dma_start(dst, src).then_inc(par_in, 16)
            act.dma_start(sinks[:, :], a["sinks"][0:1, :].partition_broadcast(P)).then_inc(small_in, 16)
            for l in range(2):
                act.dma_start(logit[:, l, :], a["ret_logit_fwd_2"][l:l + 1, :].partition_broadcast(P)).then_inc(small_in, 16)
                act.dma_start(logit[:, 2 + l, :], a["ret_logit_bwd_2"][l:l + 1, :].partition_broadcast(P)).then_inc(small_in, 16)
            for kv in range(2):
                act.dma_start(w2[:, kv], a["cmp_w2"][0, kv].rearrange("(c p) n -> p c n", p=P)).then_inc(small_in, 16)

            def norm_act(r):
                act.wait_ge(evacuated, X_READY[r])
                for k in range(2):
                    fn(u(0, P, DC, S)[:, k * HALF:(k + 1) * HALF, :], x[:, k * HALF:(k + 1) * HALF, :], ACT.Square
                       ).then_inc(*sq_ready.mark(r, k))
                act.wait_ge(*sumsq.after(r))
                if r > 0:
                    act.wait_ge(*h_ready.after(r - 1))
                chained(fn(lnx[:, :], ps[:, 5, 0:S], ACT.Ln, bias=eps, scale=1.0 / D), "ln", r)
                fn(rstd[:, :], lnx[:, :], ACT.Exp, scale=-0.5).then_inc(*rstd_ready.mark(r))

            def ffn_act(f, s0, g0, r):
                norm_act(r)
                with act.Fori(0, GU_GROUPS // 2) as i:
                    for k in range(2):
                        act.wait_ge(slab_done, i * 8 + (s0 + 4 * k + 2))
                        act.wait_ge(evacuated, i * 2 + (g0 + k - 1))
                        fn(u(SILU + 512 * k, P, 512), acc(g0 + k, 0), ACT.Silu).then_inc(silu_done, 1)

            act.wait_ge(*vec_out.after("par", 4))
            fn(cact[:, :], pcol("c_2", 0, DC), ACT.Silu).then_inc(*act_out.mark("cact"))
            act.wait_ge(small_in, SMALL)
            fn(lgt[:, 0, :], logit[:, :, :].rearrange("p a b -> p (a b)"), ACT.Abs).then_inc(*act_out.mark("labs"))
            act.wait_ge(*act_out.after("labs"))
            fn(lgt[:, 1, :], lgt[:, 0, :], ACT.Exp, scale=-1.0).then_inc(*act_out.mark("lexp"))
            ffn_act(0, S_F1, G_F1, 0)

            norm_act(1)
            act.wait_ge(*vec_out.after("gains"))
            for p in range(PROJ + 1):
                if p < PROJ and p in NORMED:
                    n = NORMED[p][1]
                    act.wait_ge(slab_done, S_MIX + 2 * p + 2)
                    back = [q for q in NORMED if q < p and (q - p) % 2 == 0]
                    if back:
                        act.wait_ge(*pe_out.after("pstat", back[-1]))
                    fn(u(SQ + (p % 2) * 512, P, n * S), acc(G_MIX + p)[:, 0:n * S], ACT.Square).then_inc(*act_out.mark("psq", p))
                q = p - 1
                if q in NORMED:
                    n = NORMED[q][1]
                    act.wait_ge(*pe_out.after("pstat", q))
                    back = [r for r in NORMED if r < q and (r - q) % 2 == 0]
                    chained(fn(u(LN + (q % 2) * 512, P, n * S), ps[:, 5, 0:n * S], ACT.Ln, bias=eps, scale=1.0 / DH), "pln", q)
                    if back:
                        act.wait_ge(*vec_out.after("qk", back[-1]))
                    fn(u(RS + (q % 2) * 512, P, n * S), u(LN + (q % 2) * 512, P, n * S), ACT.Exp, scale=-0.5).then_inc(*act_out.mark("prs", q))
                if q in VALUES:
                    v0, n = VALUES[q]
                    act.wait_ge(*pe_out.after("vt", q))
                    for c in range(n):
                        last = fn(vn[:, :, v0 + c, :], ps[:, 7, c * S:(c + 1) * S].rearrange("p (t c) -> p t c", t=TT), ACT.Copy)
                    last.then_inc(*act_out.mark("vn", q))
            sg, gg = S_MIX + 2 * PROJ, G_MIX + PROJ
            act.wait_ge(slab_done, sg + 2)
            fn(u(CTMP, 36, S), acc(gg)[0:36, 0:S], ACT.Exp, scale=-1.0).then_inc(*act_out.mark("cgate"))
            act.wait_ge(slab_done, sg + 6)
            fn(u(CHID, P, 120), ps[:, 4, 0:120], ACT.Silu).then_inc(*act_out.mark("chid"))
            act.wait_ge(*pe_out.after("gn"))
            fn(gn[:, :, :], ps[:, 7, 0:72].rearrange("p (t c) -> p t c", t=TT), ACT.Copy).then_inc(*act_out.mark("gn"))
            act.wait_ge(*pe_out.after("kcvc"))
            fn(vc[0:NCMP, :, :], ps[0:NCMP, 6, 128:256].rearrange("p (g d) -> p g d", g=2), ACT.Copy).then_inc(*act_out.mark("vc"))
            fn(kcs[:, 0, :], ps[:, 6, 64:64 + NCMP], ACT.Square).then_inc(*act_out.mark("kcsq"))
            act.wait_ge(*pe_out.after("kcstat"))
            chained(fn(kcs[:, 1, :], ps[:, 5, 0:NCMP], ACT.Ln, bias=eps, scale=1.0 / DH), "kcln")
            fn(kcs[:, 2, :], kcs[:, 1, :], ACT.Exp, scale=-0.5).then_inc(*act_out.mark("kcrs"))

            def exps(un):
                act.wait_ge(*biased.after(un["key"]))
                for i, sm in enumerate(un["softmax"]):
                    last = fn(ebuf[:, un["e"], sm["col"]:sm["col"] + sm["n"]], ebuf[:, un["e"], sm["col"]:sm["col"] + sm["n"]],
                              ACT.Exp, bias=negmax[:, un["e"], i:i + 1], accum_out=den[:, un["e"], i:i + 1])
                last.then_inc(*expd.mark(un["key"]))

            def pt_copies(un):
                act.wait_ge(*ptr.after(un["key"]))
                if un["prev"] is not None:
                    act.wait_ge(*pv.after(un["prev"]))
                full = sum(b["n"] == P for b in un["blocks"])
                last = fn(pT[:, 0:4 * P], ps[:, 1, :], ACT.Copy)
                if full > 4:
                    w = min(full, 8) - 4
                    last = fn(pT[:, 4 * P:(4 + w) * P], ps[:, 7, 0:w * P], ACT.Copy)
                if full > 8:
                    last = fn(pT[:, 8 * P:9 * P], ps[:, 3, S:S + P], ACT.Copy)
                if full < len(un["blocks"]):
                    k = len(un["blocks"]) - full
                    last = fn(pT[0:NCMP, full * P:(full + k) * P], ps[0:NCMP, 7, (full - 4) * P:(full - 4 + k) * P], ACT.Copy)
                last.then_inc(*ptc.mark(un["key"]))

            first = units_mix()
            act.wait_ge(*vec_out.after("qk", PROJ - 1))
            act.wait_ge(*vec_out.after("kc"))
            for step in range(len(first) + 1):
                if 0 < step <= GATES:
                    p = step - 1
                    act.wait_ge(slab_done, sg + 6 + 2 * p + 2)
                    fn(merged[:, 2 * p:2 * p + 2, :], acc(gg + 1 + p), ACT.Exp, scale=-1.0).then_inc(*act_out.mark("gexp", p))
                if step < len(first):
                    exps(first[step])
                if step > 0:
                    pt_copies(first[step - 1])

            ffn_act(1, S_F2, G_F2, 2)

            for l in range(2):
                s0, g0 = S_LAY[l], G_LAY[l]
                norm_act(3 + l)
                na, ret = units_na(l), units_ret(l)
                for p in range(PIECE + 1):
                    q = p - 1
                    if q in (8, 9) or q >= 18:
                        act.wait_ge(slab_done, s0 + 2 * q + 2)
                        if q - 1 in (8, 9) or q - 1 >= 18:
                            act.wait_ge(evacuated, g0 + q)
                        fn(u(LT2, P, 512), acc(g0 + q), ACT.Exp, scale=-1.0).then_inc(*act_out.mark("lexp", l, q))
                    if 6 <= p < 14:
                        exps(na[p - 6])
                    if q in (5, 6) or q in (15, 16):
                        v = q - 1
                        which, c0 = (0 if v < 10 else 1), 2 * (v % 2)
                        act.wait_ge(*pe_out.after("lvt", l, v))
                        for c in range(2):
                            last = fn(lv[:, 2 * which:2 * which + 2, c0 + c, :],
                                      ps[:, 7, c * S:(c + 1) * S].rearrange("p (t c) -> p t c", t=TT), ACT.Copy)
                        last.then_inc(*act_out.mark("lv", l, v))
                    if 6 < p <= 14:
                        pt_copies(na[p - 7])
                    if 18 <= p < 26:
                        hh = p - 18
                        act.wait_ge(*vec_out.after("dexp", l, hh))
                        fn(ebuf[:, hh % 2, 512:1024], ebuf[:, hh % 2, 512:1024], ACT.Exp).then_inc(*act_out.mark("dec", l, hh))
                for c in range(4):
                    act.wait_ge(*pe_out.after("fy", l, c))
                    fn(fx[:, c, :], ps[:, 7, 0:S], ACT.Copy).then_inc(*act_out.mark("fy", l, c))
                act.wait_ge(*o_out.after("ret", l, 7))
                for c in range(2):
                    fn(u(LSQ + 512 * c, P, 512), u(CT + (8 + 2 * c) * S, P, 512), ACT.Square).then_inc(*act_out.mark("rsq", l, c))
                for c in range(2):
                    act.wait_ge(*pe_out.after("rstat", l, c))
                    chained(fn(u(LT1 + 512 * c, P, 512), ps[:, 5, :], ACT.Ln, bias=eps, scale=1.0 / DH), "rln", l, c)
                    fn(u(LT1 + 512 * c, P, 512), u(LT1 + 512 * c, P, 512), ACT.Exp, scale=-0.5).then_inc(*act_out.mark("rrs", l, c))
                act.wait_ge(*vec_out.after("centred", l))
                fn(u(LSQ, P, 1024), u(CY, P, 1024), ACT.Square).then_inc(*act_out.mark("ysq", l))
                act.wait_ge(*pe_out.after("var", l))
                chained(fn(lnx[:, :], ps[:, 6, 0:S], ACT.Ln, bias=eps, scale=1.0 / 512), "yln", l)
                fn(rstd[:, :], lnx[:, :], ACT.Exp, scale=-0.5).then_inc(*act_out.mark("yrs", l))
                act.wait_ge(*vec_out.after("yaff", l))
                fn(u(LT1, P, 1024), u(CY, P, 1024), ACT.Exp, scale=-1.0).then_inc(*act_out.mark("yexp", l))
            norm_act(5)

        @block.vector
        def _(dve):
            v = nc.vector

            def chained(ins, *key):
                ins.then_inc(*vec_out.mark(*key))
                dve.wait_ge(*vec_out.after(*key))

            def norm_vec(r, gain, shift=None):
                dve.wait_ge(*rstd_ready.after(r))
                if r > 0:
                    dve.wait_ge(evacuated, X_READY[r])
                for c in range(DC):
                    last = v.scalar_tensor_tensor(h[:, c, :], x[:, c, :], gain[:, c:c + 1], rstd[:, :], ALU.mult, ALU.mult)
                if shift is not None:
                    chained(last, "hs", r)
                    for c in range(DC):
                        last = v.tensor_scalar(h[:, c, :], h[:, c, :], shift[:, c:c + 1], None, ALU.add)
                last.then_inc(*h_ready.mark(r))

            def ffn_vec(f, s0, g0, r, gain):
                norm_vec(r, gain)
                with dve.Fori(0, GU_GROUPS // 2) as i:
                    for k in range(2):
                        dve.wait_ge(slab_done, i * 8 + (s0 + 4 * k + 4))
                        dve.wait_ge(silu_done, i * 2 + (GU_GROUPS * f + k + 1))
                        v.tensor_tensor(U[:, bass.ds(i * 1024 + 512 * k, 512)], acc(g0 + k, 1), u(SILU + 512 * k, P, 512),
                                        ALU.mult).then_inc(evacuated, 1)
                s1, g1 = s0 + 4 * GU_GROUPS, g0 + GU_GROUPS
                with dve.Fori(0, DOWN_GROUPS // 2) as i:
                    for k in range(2):
                        for b in range(3):
                            m = 3 * k + b
                            dve.wait_ge(ada_in[m % 2], i * 48 + 16 * (12 * f + m // 2 + 1))
                            w, total = u(ADA_RING + (m % 2) * DC * W2, P, DC, W2), u(ADA_ACC + m * W2, P, W2)
                            for c in range(DC):
                                if c == 0:
                                    ins = v.tensor_scalar(total, w[:, 0, :], cact[:, 0:1], None, ALU.mult)
                                else:
                                    dve.wait_ge(ada_step, i * 90 + (15 * (24 * f + m) + c))
                                    ins = v.scalar_tensor_tensor(total, w[:, c, :], cact[:, c:c + 1], total, ALU.mult, ALU.add)
                                ins.then_inc(ada_sum if c == DC - 1 else ada_step, 1)
                        dve.wait_ge(slab_done, i * 8 + (s1 + 4 * k + 4))
                        par_banks = ps[:, 2 * ((g1 + k) % 2):2 * ((g1 + k) % 2) + 2, 0:S]
                        xs = x[:, bass.ds(i * 4 + 2 * k, 2), :]
                        v.scalar_tensor_tensor(xs, par_banks, 0.5, xs, ALU.mult, ALU.add).then_inc(evacuated, 1)
                dve.wait_ge(ada_red, 8 * (f + 1))
                chained(v.tensor_tensor(mod[:, f, :], ps[:, 4, 0:48], pcol("b_ada_2", 48 * f, 48), ALU.add), "mod", f)
                chained(v.scalar_tensor_tensor(ascale[:, f, :], mod[:, f, 16:32], 1.0, pcol("norm_g_2", 16 * f, 16), ALU.add, ALU.mult),
                        "ascale", f)

            at = 0
            for t, tile in enumerate(PARAM_TILES):
                n = sum(w for _, w in tile)
                dve.wait_ge(*pt_done.after(len(PARAM_TILES) - 1))
                chained(v.tensor_copy(par[:, at:at + n], ps[:, 4 + t // 4, (t % 4) * P:(t % 4) * P + n]), "par", t)
                at += n
            for q in (0, 2, 4):
                last = v.tensor_scalar(pcol("qk_gain", q), pcol("qk_gain", q), DH ** -0.5, None, ALU.mult)
            last.then_inc(*vec_out.mark("gains"))
            for g in range(G_LOAD):
                dve.wait_ge(*xt.after(g))
                v.tensor_copy(x[:, 2 * g:2 * g + 2, :], acc(g)).then_inc(evacuated, 1)
            dve.wait_ge(*act_out.after("cact"))
            dve.wait_ge(*act_out.after("lexp"))
            yv, zv, wv = lgt[:, 1, :], lgt[:, 0, :], lgt[:, 2, :]
            chained(v.tensor_scalar(zv, yv, 2.0, None, ALU.add), "l0")
            chained(v.reciprocal(zv, zv), "l1")
            chained(v.tensor_tensor(zv, zv, yv, ALU.mult), "l2")
            chained(v.tensor_tensor(yv, zv, zv, ALU.mult), "l3")
            chained(v.tensor_scalar(wv, yv, 1.0 / 19, 1.0 / 17, ALU.mult, ALU.add), "l4")
            for k in range(15, 0, -2):
                chained(v.tensor_tensor(wv, wv, yv, ALU.mult), "l5", k)
                chained(v.tensor_scalar(wv, wv, 1.0 / k, None, ALU.add), "l6", k)
            chained(v.tensor_tensor(wv, wv, zv, ALU.mult), "l7")
            flat = logit[:, :, :].rearrange("p a b -> p (a b)")
            chained(v.tensor_scalar(flat, flat, 0.0, None, ALU.min), "l8")
            chained(v.scalar_tensor_tensor(flat, wv, -2.0, flat, ALU.mult, ALU.add), "l9")

            ffn_vec(0, S_F1, G_F1, 0, pcol("ffn1_norm", 0, DC))

            norm_vec(1, pcol("mix_norm", 0, DC))
            for p in range(PROJ + 1):
                if p < PROJ:
                    bank = acc(G_MIX + p)
                    dve.wait_ge(slab_done, S_MIX + 2 * p + 2)
                    done = None
                    if p in NORMED:
                        dve.wait_ge(*act_out.after("psq", p))
                    if p in VALUES:
                        n = VALUES[p][1]
                        prev = [q for q in VALUES if q < p and (q - p) % 2 == 0]
                        if prev:
                            dve.wait_ge(*pe_out.after("vt", prev[-1]))
                        done = v.tensor_copy(u(VRAW + (p % 2) * 512, P, n * S), bank[:, (2 - n) * S:2 * S])
                    if p in NORMED:
                        c0, n, row = NORMED[p]
                        done = v.tensor_scalar(qk[:, c0:c0 + n, :], bank[:, 0:n * S].rearrange("p (c s) -> p c s", c=n),
                                               pcol("qk_gain", row), None, ALU.mult)
                    if p == CMP_GROUP:
                        done = v.tensor_copy(u(CRAW, P, 512), bank)
                    done.then_inc(evacuated, 1)
                q = p - 1
                if q in NORMED:
                    c0, n, row = NORMED[q]
                    dve.wait_ge(*act_out.after("prs", q))
                    dve.wait_ge(evacuated, G_MIX + q + 1)
                    v.tensor_tensor(qk[:, c0:c0 + n, :], qk[:, c0:c0 + n, :], u(RS + (q % 2) * 512, P, n, S), ALU.mult
                                    ).then_inc(*vec_out.mark("qk", q))
                if p == CMP_GROUP + 1:
                    dve.wait_ge(evacuated, G_MIX + CMP_GROUP + 1)
                    for kv in range(2):
                        dst = u(CBLK + kv * 480, P, DC, 30)
                        for g in range(2):
                            for e in range(2):
                                at = CRAW + kv * S + e
                                one = U[g * DH:(g + 1) * DH, at:at + 1]
                                src = bass.AP(one.tensor, one.offset, [one.ap[0], [2, DC], [CMP_STRIDE, NCMP]])
                                last = v.tensor_copy(dst[e * DH:(e + 1) * DH, :, g * NCMP:(g + 1) * NCMP], src)
                    chained(last, "craw")
                    for kv in range(2):
                        dst = u(CBLK + kv * 480, P, DC, 30)
                        pos = pcol("cmp_pos", 16 * kv, 16).unsqueeze(2).broadcast_to([P, DC, 30])
                        last = v.tensor_tensor(dst, dst, pos, ALU.add)
                    last.then_inc(*vec_out.mark("cblk"))
            sg, gg = S_MIX + 2 * PROJ, G_MIX + PROJ
            dve.wait_ge(*act_out.after("cgate"))
            ct = u(CTMP, 36, S)
            ins = v.tensor_scalar(ct, ct, 1.0, None, ALU.add)
            ins.then_inc(evacuated, 1)
            dve.wait_ge(evacuated, gg + 1)
            v.reciprocal(ct, ct).then_inc(*vec_out.mark("cgate"))
            dve.wait_ge(*act_out.after("kcrs"))
            v.scalar_tensor_tensor(kc[:, :], ps[:, 6, 64:64 + NCMP], pcol("qk_gain", 5), kcs[:, 2, :], ALU.mult, ALU.mult
                                   ).then_inc(*vec_out.mark("kc"))

            def bias_of(un):
                dve.wait_ge(*scores.after(un["key"]))
                e = un["e"]
                if un["prev2"] is not None:
                    dve.wait_ge(*ptr.after(un["prev2"]))
                if "sink" in un:
                    for T, at in ((0, P), (1, 512 + S)):
                        v.tensor_copy(ebuf[:, e, at:at + 1], sinks[:, un["sink"]:un["sink"] + 1])
                for seg in un["segs"]:
                    sc = ps[:, seg["bank"], seg["col"]:seg["col"] + seg["n"]]
                    at = (seg["bank"] - 4) * 512 + seg["col"]
                    dst = ebuf[:, e, at:at + seg["n"]]
                    if seg.get("nbias") is not None:
                        last = v.tensor_tensor(dst, sc, seg["nbias"], ALU.add)
                    else:
                        last = v.scalar_tensor_tensor(dst, seg["dist"], -seg["slope"], sc, ALU.mult, ALU.add)
                chained(last, "bias", un["key"])
                for i, sm in enumerate(un["softmax"]):
                    last = v.reduce_max(negmax[:, e, i:i + 1], ebuf[:, e, sm["col"]:sm["col"] + sm["n"]], AXX, negate=True)
                last.then_inc(*biased.mark(un["key"]))

            def normalise(un):
                e, k = un["e"], len(un["softmax"])
                dve.wait_ge(*expd.after(un["key"]))
                for i, sm in enumerate(un["softmax"]):
                    if sm.get("mask") is not None:
                        cols = ebuf[:, e, sm["col"]:sm["col"] + sm["n"]]
                        chained(v.tensor_tensor(cols, cols, sm["mask"], ALU.mult), "msk", un["key"], i)
                        chained(v.reduce_sum(den[:, e, i:i + 1], cols, AXX), "msum", un["key"], i)
                if un.get("gate") is not None:
                    chained(v.tensor_scalar(den[:, e, 0:k], den[:, e, 0:k], 1e-30, None, ALU.max), "dmax", un["key"])
                chained(v.reciprocal(rden[:, e, 0:k], den[:, e, 0:k]), "rden", un["key"])
                if un.get("gate") is not None:
                    gcols = gn[:, :, 3 * un["gate"]:3 * un["gate"] + 3]
                    rv = rden[:, e, 0:6].rearrange("p (t b) -> p t b", t=TT)
                    chained(v.tensor_tensor(rv, rv, gcols, ALU.mult), "rgate", un["key"])
                for i, sm in enumerate(un["softmax"]):
                    cols = ebuf[:, e, sm["col"]:sm["col"] + sm["n"]]
                    last = v.tensor_scalar(cols, cols, rden[:, e, i:i + 1], None, ALU.mult)
                last.then_inc(*probs.mark(un["key"]))

            def head_out(un):
                dve.wait_ge(*pv.after(un["key"]))
                r0 = un["half"] * DH
                v.tensor_copy(un["out"][r0:r0 + DH, :], ps[r0:r0 + DH, 3, 0:S]).then_inc(*o_out.mark(un["key"]))

            first = units_mix()
            dve.wait_ge(*act_out.after("gn"))
            for step in range(len(first) + 2):
                if step < len(first):
                    bias_of(first[step])
                if step > 1:
                    head_out(first[step - 2])
                if 0 < step <= GATES:
                    p = step - 1
                    dve.wait_ge(*act_out.after("gexp", p))
                    G = merged[:, 2 * p:2 * p + 2, :]
                    v.tensor_scalar(G, G, 1.0, None, ALU.add).then_inc(evacuated, 1)
                    dve.wait_ge(evacuated, gg + 1 + p + 1)
                    v.reciprocal(G, G).then_inc(*vec_out.mark("gate", p))
                if step < len(first):
                    normalise(first[step])
            g, n = gg + 1 + GATES, sg + 6 + 2 * GATES
            dve.wait_ge(*vec_out.after("gate", GATES - 1))
            for br, cols, count in ((0, 1024, 2), (1, 512, 4), (2, 256, 8)):
                chunk = 0
                for _k in range(count):
                    for part in range(cols // W2):
                        dve.wait_ge(*((slab_done, n + 1) if part == cols // W2 - 1 else part_done.after(g)))
                        G = merged[:, 16 * br + chunk:16 * br + chunk + 2, :]
                        if br == 0:
                            v.tensor_tensor(G, G, acc(g).rearrange("p (c s) -> p c s", c=2), ALU.mult).then_inc(evacuated, 1)
                        else:
                            chained(v.tensor_tensor(G, G, acc(g).rearrange("p (c s) -> p c s", c=2), ALU.mult), "gp", g)
                            M = merged[:, chunk:chunk + 2, :]
                            v.tensor_tensor(M, M, G, ALU.add).then_inc(evacuated, 1)
                        chunk += 2
                        g += 1
                    n += 1
            for p in range(OUTG):
                dve.wait_ge(slab_done, n + 2 * p + 2)
                X = x[:, 2 * p:2 * p + 2, :]
                v.tensor_tensor(X, X, acc(g + p).rearrange("p (c s) -> p c s", c=2), ALU.add).then_inc(evacuated, 1)

            ffn_vec(1, S_F2, G_F2, 2, pcol("ffn2_norm", 0, DC))

            for l in range(2):
                s0, g0 = S_LAY[l], G_LAY[l]
                for b in range(8):
                    dve.wait_ge(*pe_out.after("nb", l, b))
                    dst = nbias.rearrange("p h d k -> p k (h d)")[:, 8 * b:8 * b + 8, :]
                    mask = cst("wmask")[:, 8 * b:8 * b + 8].unsqueeze(2).broadcast_to([P, 8, 48])
                    v.tensor_tensor(dst, ps[:, 6 + b % 2, 0:384].rearrange("p (k x) -> p k x", k=8), mask, ALU.add
                                    ).then_inc(*vec_out.mark("nb", l, b))
                norm_vec(3 + l, ascale[:, l, :], mod[:, l, 0:16])
                v.memset(upad, 0.0).then_inc(*vec_out.mark("pad", l))
                na, ret = units_na(l), units_ret(l)
                conv_at = 0

                def conv_chunk(c):
                    for k in range(TAPS):
                        col = pcol("conv_w_2a" if l == 0 else "conv_w_2b", 4 * k + c)
                        src = upad[:, c, k:k + S]
                        if k == 0:
                            ins = v.tensor_scalar(cy[:, c, :], src, col, pcol("conv_b_2", 4 * l + c), ALU.mult, ALU.add)
                        else:
                            ins = v.scalar_tensor_tensor(cy[:, c, :], src, col, cy[:, c, :], ALU.mult, ALU.add)
                        chained(ins, "tap", l, c, k)

                for p in range(PIECE + 2):
                    if 6 <= p < 14:
                        bias_of(na[p - 6])
                    if 8 <= p < 16:
                        head_out(na[p - 8])
                    if 18 <= p < 26:
                        hh, un = p - 18, ret[p - 18]
                        tab, lo = ebuf[:, hh % 2, 512:1024], ebuf[:, hh % 2, 0:512]
                        if hh >= 2:
                            dve.wait_ge(*pv.after("ret", l, hh - 2))
                        chained(v.tensor_scalar(lo, cst("dneg"), logit[:, 2 + l, hh:hh + 1], None, ALU.mult), "dn", l, hh)
                        v.scalar_tensor_tensor(tab, cst("dpos"), logit[:, l, hh:hh + 1], lo, ALU.mult, ALU.add
                                               ).then_inc(*vec_out.mark("dexp", l, hh))
                    q = p - 1
                    if 0 <= q < PIECE:
                        bank, k2 = acc(g0 + q), acc(g0 + q).rearrange("p (c s) -> p c s", c=2)
                        c2 = 2 * (q % 2)
                        dve.wait_ge(slab_done, s0 + 2 * q + 2)
                        if q in (0, 1):
                            ins = v.tensor_scalar(lq[:, c2:c2 + 2, :], k2, DH ** -0.5, None, ALU.mult)
                        elif q in (2, 3):
                            ins = v.tensor_copy(lq[:, 4 + c2:6 + c2, :], k2)
                        elif q in (4, 5, 14, 15):
                            ins = v.tensor_copy(u(LT1 + 512 * (q % 2), P, 512), bank)
                        elif q in (6, 7):
                            if q == 6:
                                dve.wait_ge(*vec_out.after("pad", l))
                            ins = v.tensor_copy(upad[:, c2:c2 + 2, TAPS // 2:TAPS // 2 + S], k2)
                        elif q in (8, 9):
                            e = u(LT2, P, 2, S)
                            dve.wait_ge(*act_out.after("lexp", l, q))
                            chained(v.tensor_scalar(e, e, 1.0, None, ALU.add), "s1", l, q)
                            chained(v.reciprocal(e, e), "s2", l, q)
                            mid = upad[:, c2:c2 + 2, TAPS // 2:TAPS // 2 + S]
                            ins = v.tensor_tensor(mid, mid, e, ALU.mult)
                        elif q in (10, 11):
                            ins = v.tensor_scalar(lq[:, 8 + c2:10 + c2, :], k2, DH ** -0.5, None, ALU.mult)
                        elif q in (12, 13):
                            ins = v.tensor_copy(lq[:, 12 + c2:14 + c2, :], k2)
                        elif q in (16, 17):
                            ins = v.tensor_copy(fx[:, c2:c2 + 2, :], k2)
                        else:
                            e = u(LT2, P, 2, S)
                            dve.wait_ge(*act_out.after("lexp", l, q))
                            chained(v.tensor_scalar(e, e, 1.0, None, ALU.add), "s1", l, q)
                            chained(v.reciprocal(e, e), "s2", l, q)
                            ins = v.tensor_tensor(lgate[:, 2 * (q - 18):2 * (q - 18) + 2, :], k2, e, ALU.mult)
                        ins.then_inc(evacuated, 1)
                    q = p - 2
                    if q in (10, 11, 12, 13):
                        c = 8 + 2 * (q - 10)
                        pair = lq[:, c:c + 2, :]
                        cosb = cst("cos").unsqueeze(1).broadcast_to([P, 2, S])
                        sinb = cst("sin").unsqueeze(1).broadcast_to([P, 2, S])
                        t = u(LSQ, P, 2, S)
                        dve.wait_ge(*pe_out.after("rot", l, q))
                        chained(v.tensor_tensor(t, ps[:, 6, :].rearrange("p (c s) -> p c s", c=2), sinb, ALU.mult), "rotp", l, q)
                        chained(v.tensor_tensor(pair, pair, cosb, ALU.mult), "rotc", l, q)
                        v.tensor_tensor(pair, pair, t, ALU.add).then_inc(*vec_out.mark("rotq", l, q))
                    if 14 <= p < 18:
                        if p == 14:
                            dve.wait_ge(evacuated, g0 + 10)
                        conv_chunk(p - 14)
                    if 6 <= p < 14:
                        normalise(na[p - 6])
                    if 18 <= p < 26:
                        hh = p - 18
                        un = ret[hh]
                        dve.wait_ge(*scores.after(un["key"]))
                        dve.wait_ge(*act_out.after("dec", l, hh))
                        E = ebuf[:, hh % 2, 0:512]
                        v.tensor_tensor(E.rearrange("p (c s) -> p c s", c=2), ps[:, 4:6, 0:S],
                                        ebuf[:, hh % 2, 512:1024].rearrange("p (c s) -> p c s", c=2), ALU.mult
                                        ).then_inc(*biased.mark(un["key"]))
                    if 19 <= p < 27:
                        head_out(ret[p - 19])

                for c in range(4):
                    dve.wait_ge(*pe_out.after("fp", l, c))
                    if c > 0:
                        dve.wait_ge(*pe_out.after("fy", l, c - 1))
                    v.tensor_copy(u(LT1, P, 512), ps[:, 6, :]).then_inc(*vec_out.mark("fp", l, c))
                for c in range(2):
                    dve.wait_ge(*act_out.after("rrs", l, c))
                    o = u(CT + (8 + 2 * c) * S, P, 512)
                    chained(v.tensor_tensor(o, o, u(LT1 + 512 * c, P, 512), ALU.mult), "rn", l, c)
                chained(v.tensor_tensor(cT[:, 4:12, :], cT[:, 4:12, :], lgate[:, 4:12, :], ALU.mult), "gated", l)
                dve.wait_ge(*pe_out.after("mean", l))
                mu = u(LT2, P, S)
                chained(v.tensor_scalar(mu, ps[:, 5, 0:S], 1.0 / 512, None, ALU.mult), "mu", l)
                mub = u(LT2, P, 1, S).broadcast_to([P, 4, S])
                v.tensor_tensor(cy, cy, mub, ALU.subtract).then_inc(*vec_out.mark("centred", l))
                dve.wait_ge(*act_out.after("yrs", l))
                for c in range(4):
                    last = v.scalar_tensor_tensor(cy[:, c, :], cy[:, c, :], pcol("conv_ln_g_2", 4 * l + c), rstd[:, :], ALU.mult, ALU.mult)
                chained(last, "yg", l)
                for c in range(4):
                    last = v.tensor_scalar(cy[:, c, :], cy[:, c, :], pcol("conv_ln_b_2", 4 * l + c), None, ALU.add)
                last.then_inc(*vec_out.mark("yaff", l))
                dve.wait_ge(*act_out.after("yexp", l))
                e = u(LT1, P, 1024)
                chained(v.tensor_scalar(e, e, 1.0, None, ALU.add), "y1", l)
                chained(v.reciprocal(e, e), "y2", l)
                v.tensor_tensor(u(CY, P, 1024), u(CY, P, 1024), e, ALU.mult).then_inc(*vec_out.mark("csilu", l))
                g, n = g0 + PIECE, s0 + 2 * PIECE
                for which, (o0, gate0) in enumerate(((0, 0), (12, 12))):
                    for part in range(2):
                        dve.wait_ge(*(part_done.after(g) if part == 0 else (slab_done, n + 1)))
                        ins = v.tensor_tensor(cT[:, o0 + 2 * part:o0 + 2 * part + 2, :], acc(g).rearrange("p (c s) -> p c s", c=2),
                                              lgate[:, gate0 + 2 * part:gate0 + 2 * part + 2, :], ALU.mult)
                        ins.then_inc(evacuated, 1)
                        g += 1
                    n += 1
                for p in range(OUTG):
                    dve.wait_ge(slab_done, n + 2 * p + 2)
                    v.scalar_tensor_tensor(x[:, 2 * p, :], acc(g + p)[:, 0:S], mod[:, l, 32 + 2 * p:33 + 2 * p], x[:, 2 * p, :],
                                           ALU.mult, ALU.add)
                    v.scalar_tensor_tensor(x[:, 2 * p + 1, :], acc(g + p)[:, S:2 * S], mod[:, l, 33 + 2 * p:34 + 2 * p],
                                           x[:, 2 * p + 1, :], ALU.mult, ALU.add).then_inc(evacuated, 1)
            norm_vec(5, pcol("final_g_2", 0, DC))
            for i in range(8):
                T, c4 = i // 4, i % 4
                dve.wait_ge(*pe_out.after("res", i))
                last = v.tensor_copy(u(0, P, TT, D)[:, T, c4 * 512:(c4 + 1) * 512], ps[:, i % 2, :])
                last.then_inc(*vec_out.mark("res", i))


NAMES = ["x", "ffn1_norm", "ffn1_w_gu", "ffn1_w_down", "mix_norm", "w_in", "qk_gain", "sinks", "cmp_pos", "cmp_w1",
         "cmp_w2", "w_branch_a", "w_branch_b", "w_branch_c", "w_out", "ffn2_norm", "ffn2_w_gu", "ffn2_w_down", "c_2",
         "norm_g_2", "w_ada_2", "b_ada_2", "w_in_2", "w_fft_2", "na_rel_bias_2", "ret_logit_fwd_2",
         "ret_logit_bwd_2", "conv_w_2", "conv_b_2", "conv_ln_g_2", "conv_ln_b_2", "conv_w_pw_2", "w_out_2", "final_g_2"]


def program(nc, shapes, marks, final):
    a = {n: nc.dram_tensor(f"in_{n}", shapes[n], F32, kind="ExternalInput").ap() for n in NAMES}
    const = nc.dram_tensor("in_constants", (P, CONST_COLS), F32, kind="ExternalInput").ap()
    out = nc.dram_tensor("out", (1, S, D), F32, kind="ExternalOutput").ap()
    build(nc, a, out, const, marks, final)


def kernel(**inputs):
    import concourse.bacc as bacc
    from concourse.bass_utils import run_bass_kernel_spmd
    arrays = {f"in_{n}": np.ascontiguousarray(inputs[n]) for n in NAMES}
    arrays["in_constants"] = constant_table()
    shapes = {n: arrays[f"in_{n}"].shape for n in NAMES}
    marks = {}
    program(bacc.Bacc("TRN2", target_bir_lowering=False, num_devices=1), shapes, marks, False)
    nc = bacc.Bacc("TRN2", target_bir_lowering=False, num_devices=1)
    program(nc, shapes, marks, True)
    r = run_bass_kernel_spmd(nc, [arrays], core_ids=[0])
    return r.results[0]["out"]
```

```python
from contextlib import ExitStack
from math import prod

import numpy as np
import concourse.bass as bass
from concourse import mybir

F32 = mybir.dt.float32
F32R = mybir.dt.float32r
ALU = mybir.AluOpType
ACT = mybir.ActivationFunctionType
AXX = mybir.AxisListType.X

P = 128
S = 256
TT = S // P
D = 2048
DC = D // P
FF = 5632
FC = FF // P
DH = 64
EPS = 1e-6
W2 = 2 * P
KC = 4
SLAB = KC * W2
RING = 4
SPLIT_FFN, SPLIT_MIX = 4, 3
DOWN = FC // KC
DVE_DOWN = 12
NCMP, CMP_STRIDE, CMP_END = 15, 16, 31
TAPS = 31

GU_GROUPS, DOWN_GROUPS = FF // W2, D // W2
GU_SLABS = 8 * GU_GROUPS
FFN_SLABS, FFN_GROUPS = GU_SLABS + DOWN * DOWN_GROUPS, GU_GROUPS + DOWN_GROUPS
PROJ, GATES, BRANCH, OUTG = 18, 24, 24, 8
BR_SLABS = 4 + 8 + 16
MIX_SLABS = 4 * PROJ + 4 + 8 + 4 * GATES + BR_SLABS + 4 * OUTG
MIX_GROUPS = PROJ + 1 + GATES + BRANCH + OUTG
PIECE = 26
LAY_SLABS, LAY_GROUPS = 4 * PIECE + 4 + 4 * OUTG, PIECE + 4 + OUTG
S_F1, S_MIX = 0, FFN_SLABS
S_F2 = S_MIX + MIX_SLABS
S_LAY = [S_F2 + FFN_SLABS, S_F2 + FFN_SLABS + LAY_SLABS]
G_LOAD = 8
G_F1, G_MIX = G_LOAD, G_LOAD + FFN_GROUPS
G_F2 = G_MIX + MIX_GROUPS
G_LAY = [G_F2 + FFN_GROUPS, G_F2 + FFN_GROUPS + LAY_GROUPS]
G_END = G_LAY[1] + LAY_GROUPS
X_READY = [G_F1, G_MIX, G_F2, G_LAY[0], G_LAY[1], G_END]

NORMED = {0: (0, 2, 0), 1: (2, 2, 0), 2: (4, 2, 0), 3: (6, 2, 1), 4: (8, 2, 1), 5: (10, 2, 1),
          9: (12, 2, 2), 10: (14, 2, 2), 11: (16, 1, 3), 12: (17, 2, 4), 13: (19, 2, 4), 14: (21, 2, 4),
          16: (23, 1, 5), 17: (24, 1, 5)}
VALUES = {6: (0, 2), 7: (2, 2), 8: (4, 2), 11: (6, 1), 16: (7, 1), 17: (8, 1)}
CMP_GROUP = 15
A_COLS, B_Q, C_Q, C_KV = 2304, 2304, 3072, 3840
CGATE0, GATE0 = 4608, 4644
NEG = 1e33


def slopes(n):
    return [float(v) for v in np.float32(2.0) ** (np.float32(-8.0) * np.arange(1, n + 1, dtype=np.float32) / np.float32(n))]


SL_A, SL_B, SL_C = slopes(12), slopes(8), slopes(12)

CONST, _at = {}, 0
for _name, _w in (("ident", P), ("ones", P), ("blocks", P), ("eps", 1),
                  ("dist", 5 * S), ("cdist", 2 * NCMP), ("cmask", 2 * NCMP),
                  ("cos", S), ("sin", S), ("rot", P), ("dpos", 2 * S), ("dneg", 2 * S),
                  ("dft", 2 * P), ("dcos", 2 * S), ("dsin", 2 * S), ("strip", 191), ("wmask", DH)):
    CONST[_name] = (_at, _at + _w)
    _at += _w
CONST_COLS = _at
PIECES = (2, 3, 4, 10, 11, 6, 7, 8, 0, 1, 5, 9, 12)
BASE_END, MIX_END = CONST["eps"][1], CONST["cmask"][1]


def constant_table():
    c = np.zeros((P, CONST_COLS), np.float32)

    def put(name, value):
        a, b = CONST[name]
        c[:value.shape[0], a:b] = value

    p = np.arange(P)
    put("ident", np.eye(P))
    put("ones", np.ones((P, P)))
    put("blocks", (p[:, None] // DH == p[None, :] // DH).astype(float))
    put("eps", np.full((P, 1), EPS))
    t = np.arange(S)
    d = t[:, None] - t[None, :]

    def tiles(keep, dist=d):
        m = np.where(keep, dist, NEG)
        return m[P:, :]

    put("dist", np.concatenate([tiles((d >= 0) & (d <= 128)), tiles((d >= 0) & (d % 4 == 0)),
                                tiles((d >= 0) & (d % 16 == 0)), tiles((d >= 0) & (d <= 127)),
                                tiles(d >= 0)], axis=1))
    dc = t[:, None] - (CMP_STRIDE * np.arange(NCMP) + CMP_END)[None, :]
    put("cdist", np.concatenate([np.where(dc >= 0, dc, NEG)[:P], np.where(dc >= 0, dc, NEG)[P:]], 1))
    put("cmask", np.concatenate([(dc >= 0)[:P], (dc >= 0)[P:]], 1).astype(float))
    half = DH // 2
    inv = np.float32(10000.0) ** (-np.arange(half, dtype=np.float32) / np.float32(half))
    ang = (t.astype(np.float32)[:, None] * inv[None, :]).astype(np.float64)
    put("cos", np.cos(ang).T[p % half])
    put("sin", np.sin(ang).T[p % half])
    rot = np.zeros((P, P))
    for m in range(P):
        first = m % DH < half
        rot[m + half if first else m - half, m] = -1.0 if first else 1.0
    put("rot", rot)
    dts = (t[None, :] - t[:, None]).astype(float)
    put("dpos", np.concatenate([np.maximum(dts, 0)[:P], np.maximum(dts, 0)[P:]], 1))
    put("dneg", np.concatenate([np.maximum(-dts, 0)[:P], np.maximum(-dts, 0)[P:]], 1))
    a = 2 * np.pi * np.outer(p, p) / P
    put("dft", np.concatenate([np.cos(a), np.sin(a)], 1))
    a = 2 * np.pi * (np.outer(t, t) % S) / S
    n = 1 / np.sqrt(S * P)
    put("dcos", np.concatenate([n * np.cos(a)[:P], n * np.cos(a)[P:]], 1))
    put("dsin", np.concatenate([-n * np.sin(a)[:P], -n * np.sin(a)[P:]], 1))
    strip = np.zeros((62, 191))
    for r in range(2):
        for j in range(31):
            strip[31 * r + j, 78 - j + DH * r] = 1.0
    put("strip", strip)
    col = p % DH
    start = np.clip(col - 8, 0, DH - 16)
    kc = np.arange(DH)
    put("wmask", np.where((kc[None] >= start[:, None]) & (kc[None] < start[:, None] + 16), 0.0, -1e30))
    return c


PARAM_TILES = [
    [("ffn1_norm", 16), ("mix_norm", 16), ("ffn2_norm", 16), ("cmp_pos", 32), ("qk_gain", 6)],
    [("norm_g_2", 32), ("b_ada_2", 96)],
    [("conv_w_2a", 124)], [("conv_w_2b", 124)],
    [("conv_b_2", 8), ("conv_ln_g_2", 8), ("conv_ln_b_2", 8), ("final_g_2", 16), ("c_2", 16)],
]
PCOL, _at = {}, 0
for _tile in PARAM_TILES:
    for _name, _w in _tile:
        PCOL[_name] = _at
        _at += _w
PARAMS = _at

SCR = 2 * SLAB
AT = 2 * SLAB
SILU = AT + 2 * FC * S
FTMP = SILU + 2 * 512
ADA_RING = FTMP + 512
ADA_ACC = ADA_RING + 2 * SLAB
QK, VN = 0, 25 * S
GT = VN + TT * 9 * P
SQ, LN, RS, VRAW = GT, GT + 1024, GT + 2048, GT + 3072
CRAW, CBLK, CHID = GT + 4096, GT + 4608, GT + 5568
CTMP = CHID + 4 * 2 * NCMP
W2C = GT + 8192
OT = GT + 48 * S
T1 = 384
EW = T1 + 3 * S
EB = OT + 12 * S
PT = EB + 2 * EW
DIST = PT + 9 * P
LQ, LV = 0, 16 * S
FX = LV + 2 * TT * 4 * P
LG = FX + 4 * S
CT = LG + 16 * S
UPAD = CT + 8 * S
UW = S + TAPS - 1
CY = UPAD + 4 * UW
NB = CY + 4 * S
LSQ = NB + 48 * DH
LT1, LT2 = LSQ + 1024, LSQ + 2048
LEB = LT2 + 1024
LPT = LEB + 2048
TAP0, TAPN = 10, 12
GATED = NB
LATE_AT = SILU
RB = DIST + MIX_END - BASE_END
UN = RB + 96
LNX = LPT
RES = 8192
assert LPT + 512 <= LATE_AT
assert LATE_AT + CONST_COLS - MIX_END <= RB and ADA_ACC + 2 * W2 <= RB


class Signal:

    def __init__(self, handle, marks, final):
        self.handle, self.marks, self.final, self.n = handle, marks, final, 0

    def mark(self, *key):
        key = key[0] if len(key) == 1 else key
        self.n += 1
        self.marks[key] = self.n
        return self.handle, 1

    def after(self, *key):
        key = key[0] if len(key) == 1 else key
        return self.handle, self.marks[key] if self.final else 1


def build(nc, a, out, const, marks, final):
    ctx = ExitStack()
    with ctx:
        def sb(name, shape):
            return ctx.enter_context(nc.sbuf_tensor(name, shape, F32))

        def sbr(name, shape):
            return ctx.enter_context(nc.sbuf_tensor(name, shape, F32R))

        def sem(name):
            return ctx.enter_context(nc.semaphore(name))

        def signal(name):
            return Signal(sem(name), marks.setdefault(name, {}), final)

        x = sb("x_res", [P, DC, S])
        hx = sbr("h_split", [P, 2, DC, S])
        stage = sb("stage", [P, RING, SLAB])
        base = sb("base_consts", [P, BASE_END])
        par = sb("params", [P, PARAMS])
        mod = sb("mod", [P, 2, 48])
        ascale = sb("ascale", [P, 2, DC])
        rstd = sb("rstd", [P, S])
        cact = sb("cact", [P, DC])
        sinks = sb("sinks_b", [P, 8])
        logit = sb("logit_b", [P, 4, 8])
        negmax = sb("negmax", [P, 2, 6])
        den = sb("den", [P, 2, 6])
        rden = sb("rden", [P, 2, 6])
        gn = sb("gn", [P, TT, 36])
        kc = sb("kc", [P, NCMP])
        vc = sb("vc", [P, 2, DH])
        kcs = sb("kcs", [P, 3, NCMP])
        arena = sb("arena", [P, 3 * 2 * SLAB + UN])
        arena_at = nc.sbuf_base - (3 * 2 * SLAB + UN) * 4

        def over(name, shape, dtype, at):
            return nc.alloc_sbuf_tensor_at(name, shape, dtype, offset=arena_at + 4 * at)

        ws = over("split_slabs", [P, SPLIT_FFN, 2, SLAB], F32R, 0)
        U = over("U", [P, UN], F32, 3 * 2 * SLAB)
        ats = over("act_split", [P, 2, FC * S], F32R, 3 * 2 * SLAB + AT)
        osp = over("heads_split", [P, 2, 12, S], F32R, 3 * 2 * SLAB + QK)
        ps = ctx.enter_context(nc.psum_tensor("ps", [P, 8, 512], F32))

        def u(start, *shape):
            v = U[0:shape[0], start:start + prod(shape[1:])]
            if len(shape) == 3:
                v = v.rearrange("p (a b) -> p a b", a=shape[1])
            if len(shape) == 4:
                v = v.rearrange("p (a b c) -> p a b c", a=shape[1], b=shape[2])
            return v

        def cst(name, rows=P):
            lo, hi = CONST[name]
            if hi <= BASE_END:
                return base[0:rows, lo:hi]
            at = DIST + lo - BASE_END if hi <= MIX_END else LATE_AT + lo - MIX_END
            return U[0:rows, at:at + hi - lo]

        def pcol(name, j=0, n=1):
            return par[:, PCOL[name] + j:PCOL[name] + j + n]

        ident, ones, blocks, eps = cst("ident"), cst("ones"), cst("blocks"), cst("eps")
        lnx = u(LNX, P, S)
        lgt, w2 = u(RES, P, 3, 32), u(W2C, P, 2, 2, DH)
        scr = u(SCR, P, DC, S)

        def squares(r):
            at = LSQ if r >= 4 else SILU
            return u(at, P, 512), u(at + 512, P, 512)
        merged = u(GT, P, 48, S)
        qk, vn = u(QK, P, 25, S), u(VN, P, TT, 9, P)
        oT = u(OT, P, 12, S)
        ebufs = {"mix": u(EB, P, 2, EW), "na": u(LEB, P, 2, 1024), "ret": u(LEB, P, 2, 1024)}
        pts = {"mix": u(PT, P, 9 * P), "na": u(LPT, P, 4 * P)}
        lq, lv = u(LQ, P, 16, S), u(LV, P, 2 * TT, 4, P)
        lgate, cT, cy = u(LG, P, 16, S), u(CT, P, 8, S), u(CY, P, 4, S)
        upad, fx = u(UPAD, P, 4, UW), u(FX, P, 4, S)
        nbias = u(NB, P, 8, 6, DH)

        const_in, par_in, mix_in, rb_in, late_in, small_in, out_done = (sem(n) for n in (
            "const_in", "par_in", "mix_in", "rb_in", "late_in", "small_in", "out_done"))
        x_in = [sem(f"x_in{k}") for k in range(2)]
        slab_in = [sem(f"slab_in{k}") for k in range(RING)]
        ada_in = [sem(f"ada_in{k}") for k in range(2)]
        slab_done = sem("slab_done")
        evacuated = sem("evacuated")
        silu_done = sem("silu_done")
        hi_done, lo_done = sem("hi_done"), sem("lo_done")
        act_split = sem("act_split")
        ada_step, ada_quarter, ada_red = sem("ada_step"), sem("ada_quarter"), sem("ada_red")
        sq_step = sem("sq_step")
        h_ready, sumsq, rstd_ready, scaled, rounded = (signal(n) for n in (
            "h_ready", "sumsq", "rstd_ready", "scaled", "rounded"))
        heads_ready, merged_ready = signal("heads_ready"), signal("merged_ready")
        xt, pt_done, par_ready = signal("x_transposed"), signal("params_transposed"), signal("params_ready")
        gp_done = signal("gpsimd_done")
        pe_out = signal("small_products")
        act_out = signal("act_results")
        vec_out = signal("vector_results")
        part_done = signal("branch_part")
        scores, biased, expd, probs = (signal(n) for n in ("scores", "biased", "exponentials", "probs"))
        ptr, ptc, pv, o_out = (signal(n) for n in ("probs_transposed", "probs_copied", "values_summed", "heads_out"))

        slabs = []

        def rows(w, chunk0, n):
            return w.rearrange("(c p) n -> p c n", p=P)[:, chunk0:chunk0 + n, :]

        plain = set()

        def stage_view(n, chunks, cols):
            return stage[:, n % RING, 0:chunks * cols].rearrange("p (c w) -> p c w", c=chunks)

        def quarters(w, col, split=True):
            for k in range(DC // KC):
                n = len(slabs)
                slabs.append([(stage_view(n, KC, W2), rows(w, k * KC, KC)[:, :, col:col + W2])])
                if not split:
                    plain.add(n)

        def paired_heads(w, col, per, j0):
            for k in range(DC // KC):
                n = len(slabs)
                view = stage_view(n, KC, W2)
                src = rows(w, k * KC, KC)[:, :, col:col + 2 * per * DH].rearrange("p c (g j d) -> p c g j d", g=2, j=per)
                slabs.append([(view[:, :, (2 * j + g) * DH:(2 * j + g + 1) * DH], src[:, :, g, j0 + j, :])
                              for j in range(2) for g in range(2)])

        def down_slabs(w):
            for g in range(DOWN_GROUPS):
                for k in range(DOWN):
                    n = len(slabs)
                    slabs.append([(stage_view(n, KC, W2), rows(w, k * KC, KC)[:, :, g * W2:(g + 1) * W2])])

        def stream():
            for j in range(GU_GROUPS):
                quarters(a["ffn1_w_gu"][0], j * W2)
                quarters(a["ffn1_w_gu"][0], FF + j * W2)
            down_slabs(a["ffn1_w_down"][0])
            w_in = a["w_in"][0]
            for p in range(PROJ):
                if p in (9, 10):
                    paired_heads(w_in, B_Q, 4, 2 * (p - 9))
                elif p in (12, 13, 14):
                    paired_heads(w_in, C_Q, 6, 2 * (p - 12))
                else:
                    quarters(w_in, p * W2)
            quarters(w_in, CGATE0)
            for kv in range(2):
                quarters(a["cmp_w1"][0, kv], 0, split=False)
            for p in range(GATES):
                quarters(w_in, GATE0 + p * W2)
            for k in range(4):
                n = len(slabs)
                slabs.append([(stage_view(n, 2, 512), rows(a["w_branch_a"][0], 0, 2)[:, :, k * 512:(k + 1) * 512])])
            for w, per, kc_ in ((a["w_branch_b"][0], 4, 4), (a["w_branch_c"][0], 6, 3)):
                src = w.rearrange("(g j d) n -> g d j n", g=2, j=per)
                for k in range(D // W2):
                    for j0 in range(0, per, kc_):
                        n = len(slabs)
                        v = stage_view(n, kc_, W2)
                        slabs.append([(v[g * DH:(g + 1) * DH], src[g][:, j0:j0 + kc_, k * W2:(k + 1) * W2]) for g in range(2)])
            for p in range(OUTG):
                quarters(a["w_out"][0], p * W2)
            for j in range(GU_GROUPS):
                quarters(a["ffn2_w_gu"][0], j * W2)
                quarters(a["ffn2_w_gu"][0], FF + j * W2)
            down_slabs(a["ffn2_w_down"][0])
            for l in range(2):
                for piece in PIECES:
                    for k in range(2):
                        quarters(a["w_in_2"][l], piece * 512 + k * W2)
                for w in (a["w_fft_2"][l], a["conv_w_pw_2"][l]):
                    for k in range(2):
                        n = len(slabs)
                        slabs.append([(stage_view(n, KC, W2), rows(w, 0, KC)[:, :, k * W2:(k + 1) * W2])])
                        plain.add(n)
                for p in range(OUTG):
                    quarters(a["w_out_2"][l], p * W2)

        stream()
        assert len(slabs) == S_LAY[1] + LAY_SLABS
        loaded, _count = [], [0] * RING
        for n, parts in enumerate(slabs):
            _count[n % RING] += 16 * len(parts)
            loaded.append(_count[n % RING])
        nth, slot, before, _user, _k, _last = {}, {}, {}, {}, 0, None
        last_branch = S_F2 - 4 * OUTG - 1
        for n in range(len(slabs)):
            if n in (S_F1, S_MIX, S_F2, S_LAY[0]):
                _k = 0
            if n in plain:
                continue
            ring_n = SPLIT_FFN if n < S_MIX or S_F2 <= n < S_LAY[0] else SPLIT_MIX
            nth[n], slot[n] = len(nth) + 1, _k % ring_n
            before[n] = last_branch if n == S_F2 + 3 else _user.get(slot[n])
            _user[slot[n]] = n
            _k += 1

        def slab_loaded(n):
            return slab_in[n % RING], loaded[n]

        def released(n):
            return (slab_done, n + 1) if n in plain else (lo_done, nth[n])

        def slab_part(n, which, width=SLAB):
            return ws[:, slot[n], which, 0:width]

        def size(n):
            return sum(prod(dst.shape[1:]) * dst.shape[0] for dst, _ in slabs[n]) // P

        def acc(g, side=0):
            return ps[:, 2 * (g % 2) + side, :]

        def pt_bank(i):
            return ps[:, 1 if i < 4 else 7, (i % 4) * P:(i % 4 + 1) * P] if i < 8 else ps[:, 3, S:S + P]

        dist = cst("dist").rearrange("p (t c) -> p t c", t=5)

        def dist_of(table, T):
            return dist[:, table, P:S] if T == 0 else dist[:, table, :]

        def segment(T, bank, col, ecol, n, q, k, half, **more):
            return dict(T=T, bank=bank, col=col, ecol=ecol, n=n, q=q, k=k, half=half, **more)

        def block_of(T, col, n, val):
            return dict(T=T, col=col, n=n, v=val)

        def finish(units, name):
            for i, un in enumerate(units):
                un["key"] = (*name, i)
                un["prev"] = units[i - 1]["key"] if i else None
                un["prev2"] = units[i - 2]["key"] if i > 1 else None
                un["e"], un["E"], un["pT"] = i % 2, ebufs[name[0]], pts.get(name[0])
                for T in range(TT):
                    mine = [b for b in un["blocks"] if b["T"] == T]
                    for b in mine:
                        b["first"], b["last"] = b is mine[0], b is mine[-1]
            return units

        def units_mix():
            units = []
            for hh in range(4):
                half, c = hh % 2, [(4 * g + hh) // 2 for g in range(3)]
                vcols = slice(half * DH, half * DH + DH)
                segs = [segment(0, 4, g * P, g * P, P, qk[:, c[g], :], qk[:, 6 + c[g], :], half, dist=dist_of(g, 0), slope=SL_A[4 * g + hh])
                        for g in range(3)]
                segs += [segment(1, 5 + g // 2, (g % 2) * S, T1 + g * S, S, qk[:, c[g], :], qk[:, 6 + c[g], :], half, dist=dist_of(g, 1),
                                 slope=SL_A[4 * g + hh]) for g in range(3)]
                blks = [block_of(0, g * P, P, vn[:, 0, c[g], vcols]) for g in range(3)]
                blks += [block_of(1, T1 + g * S + kb * P, P, vn[:, kb, c[g], vcols]) for g in range(3) for kb in range(TT)]
                units.append(dict(segs=segs, blocks=blks, half=half, out=oT[:, hh // 2, :],
                                  softmax=[dict(col=0, n=384), dict(col=T1, n=768)]))
            for hh in range(8):
                j, g = hh % 4, hh // 4
                vcols = slice(g * DH, g * DH + DH)
                segs = [segment(T, 4 + T, 0, T1 * T, (T + 1) * P, qk[:, 12 + j, :], qk[:, 16, :], g, dist=dist_of(3, T), slope=SL_B[hh])
                        for T in range(TT)]
                blks = [block_of(T, T1 * T + kb * P, P, vn[:, kb, 6, vcols]) for T in range(TT) for kb in range(T + 1)]
                units.append(dict(segs=segs, blocks=blks, half=g, out=oT[:, 2 + j, :], sink=hh,
                                  softmax=[dict(col=0, n=P + 1), dict(col=T1, n=S + 1)]))
            for hh in range(12):
                j, g = hh % 6, hh // 6
                vcols = slice(g * DH, g * DH + DH)
                q = qk[:, 17 + j, :]
                segs, soft, blks, cmps = [], [], [], []
                for T in range(TT):
                    n, e0 = (T + 1) * P, T1 * T
                    cb, cc = (4, S) if T == 0 else (6, 0)
                    ce = e0 + 2 * n
                    for i in range(2):
                        segs.append(segment(T, 4 + T, i * n, e0 + i * n, n, q, qk[:, 23 + i, :], g, dist=dist_of(4, T), slope=SL_C[hh]))
                    segs.append(segment(T, cb, cc, ce, NCMP, q, kc[:, :], g, dist=cst("cdist")[:, T * NCMP:(T + 1) * NCMP], slope=SL_C[hh]))
                    soft += [dict(col=ce, n=NCMP, mask=cst("cmask")[:, T * NCMP:(T + 1) * NCMP]), dict(col=e0, n=n), dict(col=e0 + n, n=n)]
                    blks += [block_of(T, e0 + i * n + kb * P, P, vn[:, kb, 7 + i, vcols]) for i in range(2) for kb in range(T + 1)]
                    cmps.append(block_of(T, ce, NCMP, vc[0:NCMP, g, :]))
                units.append(dict(segs=segs, blocks=blks + cmps, half=g, out=oT[:, 6 + j, :], gate=hh, softmax=soft))
            return finish(units, ("mix",))

        def units_na(l):
            units = []
            for hh in range(8):
                half, c = hh % 2, hh // 2
                vcols = slice(half * DH, half * DH + DH)
                segs = [segment(T, 4 + T, 0, 512 * T, S, lq[:, c, :], lq[:, 4 + c, :], half,
                                nbias=nbias[:, hh, 2 - 2 * T:6 - 2 * T, :].rearrange("p a b -> p (a b)")) for T in range(TT)]
                blks = [block_of(T, 512 * T + kb * P, P, lv[:, kb, c, vcols]) for T in range(TT) for kb in range(TT)]
                units.append(dict(segs=segs, blocks=blks, half=half, out=cT[:, c, :],
                                  softmax=[dict(col=0, n=S), dict(col=512, n=S)]))
            return finish(units, ("na", l))

        def units_ret(l):
            units = []
            for hh in range(8):
                half, c = hh % 2, hh // 2
                vcols = slice(half * DH, half * DH + DH)
                segs = [segment(st, 4 + st, 0, st * S, S, lq[:, 12 + c, :], lq[:, 8 + c, :], half) for st in range(TT)]
                units.append(dict(segs=segs, blocks=[], half=half, head=hh, out=cT[:, 4 + c, :],
                                  v=[lv[:, TT + st, c, vcols] for st in range(TT)],
                                  before=("ret", l, hh - 1) if hh else ("na", l, 7)))
            return finish(units, ("ret", l))

        rowbuf = u(4096, P, 5, P)

        def param_rows(t, r0, src):
            n, w = src.shape
            return rowbuf[r0:r0 + n, t, 0:w], src

        by_rows = lambda ap: ap.rearrange("(r c) -> r c", c=P)
        PAR_LOADS = [param_rows(0, 0, by_rows(a["ffn1_norm"][0])), param_rows(0, 16, by_rows(a["mix_norm"][0])),
                     param_rows(0, 32, by_rows(a["ffn2_norm"][0]))]
        PAR_LOADS += [param_rows(0, 48 + 16 * kv, a["cmp_pos"][0, kv].rearrange("(c e) d -> c (e d)", e=2)) for kv in range(2)]
        gains = a["qk_gain"][0].rearrange("a b d -> (a b) d")
        PAR_LOADS += [(rowbuf[80:86, 0, k * DH:(k + 1) * DH], gains) for k in range(2)]
        PAR_LOADS += [param_rows(1, 16 * l, by_rows(a["norm_g_2"][l])) for l in range(2)]
        PAR_LOADS += [param_rows(1, 32 + 48 * l, by_rows(a["b_ada_2"][l])) for l in range(2)]
        PAR_LOADS += [param_rows(2 + l, 0, a["conv_w_2"][l].rearrange("t (c p) -> (t c) p", p=P)) for l in range(2)]
        for k, name in enumerate(("conv_b_2", "conv_ln_g_2", "conv_ln_b_2")):
            PAR_LOADS += [param_rows(4, 8 * k + 4 * l, by_rows(a[name][l])) for l in range(2)]
        PAR_LOADS += [param_rows(4, 24, by_rows(a["final_g_2"])), param_rows(4, 40, by_rows(a["c_2"][0]))]
        N_PAR = len(PAR_LOADS)
        SMALL, MIXC, BIAS = 16 * 5, 16 * 3, 16 * 32

        block = ctx.enter_context(nc.Block())

        @block.sync
        def _(sp):
            for k in range(2):
                for T in range(TT):
                    cols = slice(k * (D // 2), (k + 1) * (D // 2))
                    sp.dma_start(u(0, P, TT, D)[:, T, cols], a["x"][0, T * P:(T + 1) * P, cols]).then_inc(x_in[k], 16)

            def load(n):
                if n >= RING:
                    sp.wait_ge(*released(n - RING))
                for dst, src in slabs[n]:
                    sp.dma_start(dst, src).then_inc(slab_in[n % RING], 16)

            def load_ffn(w_gu, w_down, s0):
                for n in range(s0, s0 + 16):
                    load(n)
                    if n == S_F1 + 7:
                        for ll in range(2):
                            for r in range(2):
                                src = a["na_rel_bias_2"][ll, :, 5 - r:11 - r, :].rearrange("h d j -> j h d")
                                dst = u(RB, P, 2, 8, 6)[31 * r:31 * r + 31, ll]
                                for hh in range(8):
                                    sp.dma_start(dst[:, hh, :], src[:, hh, :], allow_slow_non_contiguous=True).then_inc(rb_in, 16)
                with sp.Fori(1, GU_GROUPS // 2) as i:
                    for k in range(16):
                        n = s0 + k
                        col = (k // 8) * W2 + (FF if k % 8 >= 4 else 0)
                        at = sp.snap(i * (2 * W2) + col)
                        sp.wait_ge(lo_done, i * 16 + (nth[s0] + k - RING))
                        sp.dma_start(stage_view(n, KC, W2), rows(w_gu, (k % 4) * KC, KC)[:, :, bass.ds(at, W2)]
                                     ).then_inc(slab_in[n % RING], 16)
                s1 = s0 + GU_SLABS
                with sp.Fori(0, 2) as i:
                    for k in range(4 * DOWN):
                        n = s1 + k
                        at = sp.snap(i * (4 * W2) + (k // DOWN) * W2)
                        sp.wait_ge(lo_done, i * (4 * DOWN) + (nth[n] - RING))
                        sp.dma_start(stage_view(n, KC, W2), rows(w_down, (k % DOWN) * KC, KC)[:, :, bass.ds(at, W2)]
                                     ).then_inc(slab_in[n % RING], 16)

            load_ffn(a["ffn1_w_gu"][0], a["ffn1_w_down"][0], S_F1)
            for n in range(S_MIX, S_F2):
                load(n)
            load_ffn(a["ffn2_w_gu"][0], a["ffn2_w_down"][0], S_F2)
            for n in range(S_LAY[0], S_LAY[1] + LAY_SLABS):
                load(n)
            for T in range(TT):
                sp.wait_ge(*vec_out.after("res", 4 * T + 3))
                sp.dma_start(out[0, T * P:(T + 1) * P, :], u(RES, P, TT, D)[:, T, :]).then_inc(out_done, 16)
            sp.wait_ge(out_done, 32)

        @block.gpsimd
        def _(pool):
            def rest(n, wait=True):
                if wait:
                    pool.wait_ge(hi_done, nth[n])
                return nc.gpsimd.tensor_tensor(slab_part(n, 1, size(n)), stage[:, n % RING, 0:size(n)],
                                               slab_part(n, 0, size(n)).bitcast(F32), ALU.subtract)

            for f, (s0, s_next, s_end) in enumerate(((S_F1, S_MIX, S_F2 + 4), (S_F2, S_LAY[0], S_LAY[1] + LAY_SLABS))):
                w = a["w_ada_2"][f].rearrange("(c p) n -> p c n", p=P)
                ring = u(ADA_RING, P, 2, SLAB)
                if f == 0:
                    for n in range(s0, s0 + 4):
                        rest(n).then_inc(lo_done, 1)
                if f == 1:
                    pool.wait_ge(evacuated, G_F2)
                for q in range(4):
                    if q >= 2 or f == 1:
                        pool.wait_ge(ada_quarter, 96 * f + q - 1)
                    pool.dma_start(ring[:, q % 2, :].rearrange("p (c w) -> p c w", c=KC), w[:, q * KC:(q + 1) * KC, 0:W2]
                                   ).then_inc(ada_in[q % 2], 16)
                with pool.Fori(1, 24) as i:
                    for q in range(4):
                        pool.wait_ge(ada_quarter, i * 4 + (96 * f + q - 1))
                        pool.dma_start(ring[:, q % 2, :].rearrange("p (c w) -> p c w", c=KC),
                                       w[:, q * KC:(q + 1) * KC, bass.ds(i * W2, W2)]).then_inc(ada_in[q % 2], 16)
                n0 = s0 + GU_SLABS + DVE_DOWN
                pool.wait_ge(lo_done, nth[n0] - 1)
                with pool.Fori(0, (DOWN * DOWN_GROUPS - DVE_DOWN) // 4) as i:
                    for k in range(4):
                        pool.wait_ge(hi_done, i * 4 + nth[n0 + k])
                        rest(n0 + k, wait=False).then_inc(lo_done, 1)
                pool.wait_ge(ada_red, f + 1)
                if f == 0:
                    pool.dma_start(U[:, DIST:DIST + MIX_END - BASE_END], const[:, BASE_END:MIX_END]).then_inc(mix_in, 16)
                    for kv in range(2):
                        pool.dma_start(w2[:, kv], a["cmp_w2"][0, kv].rearrange("(c p) n -> p c n", p=P)).then_inc(mix_in, 16)
                for n in range(s_next, s_end):
                    if f == 1 and n == s_next + 3:
                        pool.wait_ge(*sumsq.after(3))
                        pool.dma_start(U[:, LATE_AT:LATE_AT + CONST_COLS - MIX_END], const[:, MIX_END:CONST_COLS]
                                       ).then_inc(late_in, 16)
                    if n not in plain:
                        rest(n).then_inc(lo_done, 1)

        @block.tensor
        def _(pe):
            mm = nc.tensor.matmul

            def transpose(dst, src):
                n = src.shape[0]
                return nc.tensor.transpose(dst, src, ident[0:n, 0:n])

            def split_passes(bank, n, moving, first, last, chunks=KC, width=W2, col0=0, outs=2):
                w = [slab_part(n, i, chunks * width).rearrange("p (c w) -> p c w", c=chunks) for i in range(2)]
                for c in range(outs):
                    for kk in range(chunks):
                        for i, (wp, mp) in enumerate(((0, 0), (0, 1), (1, 0))):
                            at = col0 + c * P
                            ins = mm(bank[:, c * S:(c + 1) * S], w[wp][:, kk, at:at + P], moving(kk, mp),
                                     start=first and c == 0 and kk == 0 and i == 0, stop=last and c == outs - 1 and kk == chunks - 1 and i == 2)
                return ins

            def chunks_of(t, k, n=KC):
                return lambda kk, i: t[:, i, n * k + kk, :]

            def product(g, n, waits=None, outs=2, midway=None):
                pe.wait_ge(evacuated, g - 1)
                for k in range(4):
                    pe.wait_ge(lo_done, nth[n + k])
                    if waits is not None:
                        for key in waits[k]:
                            pe.wait_ge(*key)
                    split_passes(acc(g), n + k, chunks_of(hx, k), k == 0, k == 3, outs=outs).then_inc(slab_done, 1)
                    if k == 1 and midway is not None:
                        transposes_of(midway)

            def norm_waits(r):
                return [[h_ready.after(r, KC * k + KC - 1)] for k in range(4)]

            def norm_sum(r):
                pe.wait_ge(sq_step, 16 * (r + 1))
                total = squares(r)[1]
                mm(ps[:, 5, 0:S], ones, total[:, 0:S], start=True, stop=False)
                mm(ps[:, 5, 0:S], ones, total[:, S:2 * S], start=False, stop=True).then_inc(*sumsq.mark(r))

            def ada_reduce(col, b):
                for c in range(2):
                    last = mm(ps[:, 4, col(c)], u(ADA_ACC, P, 2, W2)[:, b % 2, c * P:(c + 1) * P], ones[:, 0:1],
                              start=True, stop=True)
                return last

            def ffn(f, s0, g0, r):
                norm_sum(r)
                with pe.Fori(0, GU_GROUPS // 2) as i:
                    for k in range(2):
                        pe.wait_ge(evacuated, i * 2 + (g0 + k - 1))
                        for side in range(2):
                            for q in range(4):
                                n = s0 + 8 * k + 4 * side + q
                                pe.wait_ge(lo_done, i * 16 + nth[n])
                                if k == 0 and side == 0:
                                    pe.wait_ge(*h_ready.after(r, KC * q + KC - 1))
                                split_passes(acc(g0 + k, side), n, chunks_of(hx, q), q == 0, q == 3).then_inc(slab_done, 1)
                        pe.wait_ge(ada_quarter, i * 8 + (96 * f + 4 * k + 4))
                        ada_reduce(lambda c, k=k, i=i: bass.ds(i * 4 + (2 * k + c), 1), k)
                s1, g1 = s0 + GU_SLABS, g0 + GU_GROUPS
                with pe.Fori(0, DOWN_GROUPS // 4) as i:
                    for k in range(4):
                        pe.wait_ge(evacuated, i * 4 + (g1 + k - 1))
                        for q in range(DOWN):
                            n = s1 + DOWN * k + q
                            pe.wait_ge(lo_done, i * (4 * DOWN) + nth[n])
                            if k == 0 and q in (0, DOWN - 1):
                                pe.wait_ge(act_split, 2 * GU_GROUPS * (f + 1) - (2 if q == 0 else 0))
                            at = lambda kk, j, q=q: ats[:, j, (KC * q + kk) * S:(KC * q + kk + 1) * S]
                            split_passes(acc(g1 + k), n, at, q == 0, q == DOWN - 1).then_inc(slab_done, 1)
                pe.wait_ge(ada_quarter, 96 * (f + 1))
                for b in (22, 23):
                    last = ada_reduce(lambda c, b=b: slice(2 * b + c, 2 * b + c + 1), b)
                last.then_inc(ada_red, 1)

            pe.wait_ge(const_in, 16)
            for g in range(G_LOAD):
                if g % 4 == 0:
                    pe.wait_ge(x_in[g // 4], 32)
                if g >= 2:
                    pe.wait_ge(evacuated, g - 1)
                for c in range(2):
                    for T in range(TT):
                        at = (2 * g + c) * P
                        last = transpose(acc(g)[:, c * S + T * P:c * S + (T + 1) * P], u(0, P, TT, D)[:, T, at:at + P])
                last.then_inc(*xt.mark(g))
            pe.wait_ge(par_in, 16 * N_PAR)
            for t, tile in enumerate(PARAM_TILES):
                n = sum(w for _, w in tile)
                transpose(ps[:, 6 + t // 4, (t % 4) * P:(t % 4) * P + n], rowbuf[0:n, t, :]).then_inc(*pt_done.mark(t))

            ffn(0, S_F1, G_F1, 0)

            norm_sum(1)

            def proj_lag(p):
                if p in NORMED:
                    n = NORMED[p][1]
                    pe.wait_ge(*act_out.after("psq", p))
                    if p > 0:
                        pe.wait_ge(*act_out.after("pln", max(q for q in NORMED if q < p)))
                    mm(ps[:, 5, 0:n * S], blocks, u(SQ + (p % 2) * 512, P, n * S), start=True, stop=True).then_inc(*pe_out.mark("pstat", p))
                if p in VALUES:
                    n = VALUES[p][1]
                    pe.wait_ge(evacuated, G_MIX + p + 1)
                    prev = max([q for q in VALUES if q < p], default=None)
                    if prev is not None:
                        pe.wait_ge(*act_out.after("vn", prev))
                    for c in range(n):
                        for T in range(TT):
                            last = transpose(ps[:, 7, (c * TT + T) * P:(c * TT + T + 1) * P],
                                             u(VRAW + (p % 2) * 512, P, 2, S)[:, c, T * P:(T + 1) * P])
                    last.then_inc(*pe_out.mark("vt", p))

            for p in range(PROJ):
                product(G_MIX + p, S_MIX + 4 * p, norm_waits(1) if p == 0 else None)
                if p > 0:
                    proj_lag(p - 1)
            sg, gg = S_MIX + 4 * PROJ, G_MIX + PROJ
            sA = sg + 12
            product(gg, sg, outs=1)
            proj_lag(PROJ - 1)

            pe.wait_ge(*vec_out.after("cblk"))
            for kv in range(2):
                for q in range(4):
                    n = sg + 4 + 4 * kv + q
                    pe.wait_ge(*slab_loaded(n))
                    for hc in range(2):
                        for kk in range(KC):
                            c = KC * q + kk
                            last = mm(ps[:, 4, (2 * kv + hc) * 30:(2 * kv + hc) * 30 + 30],
                                      stage_view(n, KC, W2)[:, kk, hc * P:(hc + 1) * P],
                                      u(CBLK + kv * 480, P, DC, 30)[:, c, :], start=c == 0 and hc == 0, stop=c == DC - 1 and hc == 1)
                    last.then_inc(slab_done, 1)
            pe.wait_ge(*vec_out.after("cgate"))
            for T in range(TT):
                last = transpose(ps[:, 7, T * 36:T * 36 + 36], u(CTMP, 36, S)[:, T * P:(T + 1) * P])
            last.then_inc(*pe_out.mark("gn"))
            pe.wait_ge(*act_out.after("chid"))
            pe.wait_ge(mix_in, MIXC)
            hid = u(CHID, P, 4, 2, NCMP)
            for g in range(2):
                for hc in range(2):
                    mm(ps[g * DH:(g + 1) * DH, 6, 64:64 + NCMP], w2[:, 0, hc, :], hid[:, hc, g, :], start=hc == 0, stop=hc == 1)
            for g in range(2):
                for hc in range(2):
                    last = mm(ps[0:NCMP, 6, 128 + g * DH:128 + (g + 1) * DH], hid[:, 2 + hc, g, :], w2[:, 1, hc, :],
                              start=hc == 0, stop=hc == 1)
            last.then_inc(*pe_out.mark("kcvc"))
            pe.wait_ge(*act_out.after("kcsq"))
            mm(ps[:, 5, 0:NCMP], blocks, kcs[:, 0, :], start=True, stop=True).then_inc(*pe_out.mark("kcstat"))

            def scores_of(un):
                key, segs = un["key"], un["segs"]
                if un["prev"] is not None:
                    pe.wait_ge(*biased.after(un["prev"]))
                for seg in segs:
                    rows_ = slice(seg["half"] * DH, seg["half"] * DH + DH)
                    last = mm(ps[:, seg["bank"], seg["col"]:seg["col"] + seg["n"]],
                              seg["q"][rows_, seg["T"] * P:(seg["T"] + 1) * P], seg["k"][rows_, 0:seg["n"]],
                              start=True, stop=True)
                last.then_inc(*scores.mark(key))

            def transposes_of(un):
                pe.wait_ge(*probs.after(un["key"]))
                if un["prev"] is not None:
                    pe.wait_ge(*ptc.after(un["prev"]))
                    pe.wait_ge(*o_out.after(un["prev"]))
                for i, b in enumerate(un["blocks"]):
                    last = transpose(pt_bank(i)[0:b["n"], :], un["E"][:, un["e"], b["col"]:b["col"] + b["n"]])
                last.then_inc(*ptr.mark(un["key"]))

            def values_of(un):
                pe.wait_ge(*ptc.after(un["key"]))
                for i, b in sorted(enumerate(un["blocks"]), key=lambda ib: ib[1]["T"]):
                    last = mm(ps[un["half"] * DH:(un["half"] + 1) * DH, 3, b["T"] * P:(b["T"] + 1) * P],
                              b["v"], un["pT"][0:b["n"], i * P:(i + 1) * P], start=b["first"], stop=b["last"])
                last.then_inc(*pv.mark(un["key"]))

            def decayed_values(un):
                pe.wait_ge(*biased.after(un["key"]))
                pe.wait_ge(*o_out.after(un["before"]))
                r0, hh = un["half"] * DH, un["head"]
                for st in range(TT):
                    last = mm(ps[r0:r0 + DH, 3, 0:S], un["v"][st], un["E"][:, hh % 2, st * S:(st + 1) * S],
                              start=st == 0, stop=st == TT - 1)
                last.then_inc(*pv.mark(un["key"]))

            first = units_mix()
            pe.wait_ge(*vec_out.after("qk", PROJ - 1))
            pe.wait_ge(*act_out.after("vn", PROJ - 1))
            pe.wait_ge(*vec_out.after("kc"))
            pe.wait_ge(*act_out.after("gn"))
            for step in range(len(first) + 1):
                if step < len(first):
                    scores_of(first[step])
                if step < GATES:
                    product(gg + 1 + step, sA + 4 * step, midway=first[step - 1] if step else None)
                else:
                    transposes_of(first[-1])
                if 0 < step < len(first):
                    values_of(first[step - 1])

            g, n = gg + 1 + GATES, sA + 4 * GATES
            pe.wait_ge(*heads_ready.after(0))
            for _k in range(4):
                pe.wait_ge(lo_done, nth[n])
                for half in range(2):
                    pe.wait_ge(evacuated, g - 1)
                    last = split_passes(acc(g), n, chunks_of(osp, 0, 2), True, True, chunks=2, width=512, col0=half * W2)
                    last.then_inc(*((slab_done, 1) if half == 1 else part_done.mark(g)))
                    g += 1
                n += 1
            values_of(first[-1])
            pe.wait_ge(*heads_ready.after(2))
            for _k in range(8):
                pe.wait_ge(evacuated, g - 1)
                pe.wait_ge(lo_done, nth[n])
                split_passes(acc(g), n, lambda kk, i: osp[:, i, 2 + kk, :], True, True).then_inc(slab_done, 1)
                g += 1
                n += 1
            for _k in range(8):
                pe.wait_ge(evacuated, g - 1)
                for q in range(2):
                    pe.wait_ge(lo_done, nth[n])
                    if _k == 0:
                        pe.wait_ge(*heads_ready.after(4 + q))
                    split_passes(acc(g), n, lambda kk, i, q=q: osp[:, i, 6 + 3 * q + kk, :], q == 0, q == 1, chunks=3
                                 ).then_inc(slab_done, 1)
                    n += 1
                g += 1
            for p in range(OUTG):
                product(g + p, n + 4 * p, [[merged_ready.after(2 * k + 1)] for k in range(4)] if p == 0 else None)

            ffn(1, S_F2, G_F2, 2)

            for l in range(2):
                s0, g0 = S_LAY[l], G_LAY[l]
                def neighbour_bias(b):
                    if b == 0 and l == 0:
                        pe.wait_ge(late_in, 16)
                        pe.wait_ge(rb_in, BIAS)
                    if b >= 2:
                        pe.wait_ge(*vec_out.after("nb", l, b - 2))
                    for k in range(8):
                        at = 63 - (8 * b + k)
                        last = mm(ps[:, 6 + b % 2, k * 48:(k + 1) * 48], cst("strip", 62)[:, at:at + P],
                                  u(RB, P, 2, 48)[0:62, l, :], start=True, stop=True)
                    last.then_inc(*pe_out.mark("nb", l, b))

                norm_sum(3 + l)

                def lay_lag(p):
                    if p in (10, 11, 12, 13):
                        pe.wait_ge(evacuated, g0 + p + 1)
                        if p > 10:
                            pe.wait_ge(*vec_out.after("rotp", l, p - 1))
                        mm(ps[:, 6, :], cst("rot"), u(LQ + (8 + 2 * (p - 10)) * S, P, 512), start=True, stop=True
                           ).then_inc(*pe_out.mark("rot", l, p))
                    if p in (4, 5, 14, 15):
                        pe.wait_ge(evacuated, g0 + p + 1)
                        if p in (5, 15):
                            pe.wait_ge(*act_out.after("lv", l, p - 1))
                        if p == 14:
                            pe.wait_ge(*ptc.after("na", l, 7))
                        for c in range(2):
                            for T in range(TT):
                                last = transpose(ps[:, 7, (c * TT + T) * P:(c * TT + T + 1) * P],
                                                 u(LT1, P, 2, 2, S)[:, p % 2, c, T * P:(T + 1) * P])
                        last.then_inc(*pe_out.mark("lvt", l, p))

                na, ret = units_na(l), units_ret(l)
                for p in range(PIECE):
                    if 6 <= p < 14:
                        scores_of(na[p - 6])
                    if 18 <= p:
                        if p == 18:
                            pe.wait_ge(*vec_out.after("rotq", l, 13))
                            pe.wait_ge(*act_out.after("lv", l, 15))
                        scores_of(ret[p - 18])
                    product(g0 + p, s0 + 4 * p, norm_waits(3 + l) if p == 0 else None, midway=na[p - 7] if 6 < p <= 14 else None)
                    if p < 4:
                        neighbour_bias(2 * p)
                        neighbour_bias(2 * p + 1)
                    if 6 < p <= 14:
                        if p == 7:
                            pe.wait_ge(*act_out.after("lv", l, 5))
                        values_of(na[p - 7])
                    if p > 0:
                        lay_lag(p - 1)
                    if 18 < p:
                        decayed_values(ret[p - 19])
                    if 19 <= p < 23:
                        c = p - 19
                        pe.wait_ge(*vec_out.after("fp", l, c))
                        if c > 0:
                            pe.wait_ge(*act_out.after("fy", l, c - 1))
                        fp = u(LT1, P, TT, 2, P)
                        for i, (part, tab) in enumerate(((0, "dcos"), (1, "dsin"))):
                            for T in range(TT):
                                last = mm(ps[:, 7, 0:S], fp[:, T, part, :], cst(tab)[:, T * S:(T + 1) * S],
                                          start=i == 0 and T == 0, stop=i == 1 and T == 1)
                        last.then_inc(*pe_out.mark("fy", l, c))
                    if 18 <= p < 22:
                        c = p - 18
                        if c > 0:
                            pe.wait_ge(*vec_out.after("fp", l, c - 1))
                        else:
                            pe.wait_ge(evacuated, g0 + 18)
                        for T in range(TT):
                            last = mm(ps[:, 6, T * S:(T + 1) * S], fx[:, c, T * P:(T + 1) * P], cst("dft"), start=True, stop=True)
                        last.then_inc(*pe_out.mark("fp", l, c))
                    if p == 21:
                        for c in range(4):
                            pe.wait_ge(*vec_out.after("tap", l, c, TAPS - 1))
                            last = mm(ps[:, 1, 0:S], ones, cy[:, c, :], start=c == 0, stop=c == 3)
                        last.then_inc(*pe_out.mark("mean", l))
                    if p == 22:
                        pe.wait_ge(*act_out.after("ysq", l))
                        for c in range(4):
                            last = mm(ps[:, 1, 0:S], ones, u(LSQ, P, 4, S)[:, c, :], start=c == 0, stop=c == 3)
                        last.then_inc(*pe_out.mark("var", l))
                decayed_values(ret[7])

                g, n = g0 + PIECE, s0 + 4 * PIECE
                for which, moving in ((0, fx), (1, cy)):
                    if which == 1:
                        for c in range(2):
                            pe.wait_ge(*act_out.after("rsq", l, c))
                            mm(ps[:, 6 + c, :], blocks, u(LSQ + 512 * c, P, 512), start=True, stop=True
                               ).then_inc(*pe_out.mark("rstat", l, c))
                    pe.wait_ge(*(act_out.after("fy", l, 3) if which == 0 else act_out.after("csilu", l)))
                    for _k in range(2):
                        pe.wait_ge(*slab_loaded(n))
                        pe.wait_ge(evacuated, g - 1)
                        for c in range(2):
                            for j in range(4):
                                last = mm(acc(g)[:, c * S:(c + 1) * S], stage_view(n, KC, W2)[:, j, c * P:(c + 1) * P],
                                          moving[:, j, :], start=j == 0, stop=j == 3)
                        last.then_inc(slab_done, 1)
                        g += 1
                        n += 1
                for p in range(OUTG):
                    product(g + p, n + 4 * p, [[h_ready.after("cat", l, (0, 0, 1, 2)[k])] for k in range(4)] if p == 0 else None)

            norm_sum(5)
            pe.wait_ge(*h_ready.after(5))
            for i in range(8):
                T, c4 = i // 4, i % 4
                if i >= 2:
                    pe.wait_ge(*vec_out.after("res", i - 2))
                for c in range(4):
                    last = transpose(ps[:, i % 2, c * P:(c + 1) * P], scr[:, 4 * c4 + c, T * P:(T + 1) * P])
                last.then_inc(*pe_out.mark("res", i))

        @block.scalar
        def _(act):
            fn = nc.scalar.activation

            def chained(ins, *key):
                ins.then_inc(*act_out.mark(*key))
                act.wait_ge(*act_out.after(*key))

            act.dma_start(base[:, :], const[:, 0:BASE_END]).then_inc(const_in, 16)
            for dst, src in PAR_LOADS:
                act.dma_start(dst, src).then_inc(par_in, 16)
            act.dma_start(sinks[:, :], a["sinks"][0:1, :].partition_broadcast(P)).then_inc(small_in, 16)
            for l in range(2):
                act.dma_start(logit[:, l, :], a["ret_logit_fwd_2"][l:l + 1, :].partition_broadcast(P)).then_inc(small_in, 16)
                act.dma_start(logit[:, 2 + l, :], a["ret_logit_bwd_2"][l:l + 1, :].partition_broadcast(P)).then_inc(small_in, 16)

            cursor = [0]

            def rounded_part(n):
                return fn(slab_part(n, 0, size(n)), stage[:, n % RING, 0:size(n)], ACT.Copy)

            def round_upto(n):
                while cursor[0] <= min(n, len(slabs) - 1):
                    m = cursor[0]
                    if m not in plain:
                        act.wait_ge(*slab_loaded(m))
                        if m == S_F1 + 3:
                            act.wait_ge(*xt.after(G_LOAD - 1))
                        if before[m] is not None:
                            act.wait_ge(slab_done, before[m] + 1)
                        rounded_part(m).then_inc(hi_done, 1)
                    cursor[0] += 1

            def norm_act(r, split=True, shift=None):
                act.wait_ge(*sumsq.after(r))
                chained(fn(lnx, ps[:, 5, 0:S], ACT.Ln, bias=eps, scale=1.0 / D), "ln", r)
                fn(rstd[:, :], lnx, ACT.Exp, scale=-0.5).then_inc(*rstd_ready.mark(r))
                if split:
                    for c in range(DC):
                        act.wait_ge(*scaled.after(r, c))
                        if shift is None:
                            ins = fn(hx[:, 0, c, :], scr[:, c, :], ACT.Copy)
                        else:
                            ins = fn(hx[:, 0, c, :], scr[:, c, :], ACT.Identity, bias=shift[:, c:c + 1])
                        ins.then_inc(*rounded.mark(r, c))

            def ffn_act(f, s0, g0, r):
                round_upto(s0 + 3)
                norm_act(r)
                with act.Fori(0, GU_GROUPS // 2) as i:
                    for k in range(2):
                        for q in range(8):
                            n = s0 + 8 * k + 4 + q
                            if q == 4:
                                act.wait_ge(slab_done, i * 16 + (s0 + 8 * k + 4))
                                act.wait_ge(evacuated, i * 2 + (g0 + k - 1))
                                fn(u(SILU + 512 * k, P, 512), acc(g0 + k, 0), ACT.Silu).then_inc(silu_done, 1)
                            act.wait_ge(slab_in[n % RING], i * 64 + loaded[n])
                            act.wait_ge(slab_done, i * 16 + (before[n] + 1))
                            rounded_part(n).then_inc(hi_done, 1)
                s1 = s0 + GU_SLABS
                with act.Fori(0, DOWN * DOWN_GROUPS // 4 - 1) as i:
                    for k in range(4):
                        n = s1 + 4 + k
                        act.wait_ge(slab_in[n % RING], i * 16 + loaded[n])
                        act.wait_ge(slab_done, i * 4 + (before[n] + 1))
                        rounded_part(n).then_inc(hi_done, 1)
                cursor[0] = s0 + FFN_SLABS

            act.wait_ge(*vec_out.after("par", 4))
            fn(cact[:, :], pcol("c_2", 0, DC), ACT.Silu).then_inc(*act_out.mark("cact"))
            act.wait_ge(small_in, SMALL)
            fn(lgt[:, 0, :], logit[:, :, :].rearrange("p a b -> p (a b)"), ACT.Abs).then_inc(*act_out.mark("labs"))
            act.wait_ge(*act_out.after("labs"))
            fn(lgt[:, 1, :], lgt[:, 0, :], ACT.Exp, scale=-1.0).then_inc(*act_out.mark("lexp"))
            ffn_act(0, S_F1, G_F1, 0)

            round_upto(S_MIX + 2)
            norm_act(1)
            act.wait_ge(*vec_out.after("gains"))
            for p in range(PROJ + 1):
                round_upto(S_MIX + 4 * p + 6)
                if p < PROJ and p in NORMED:
                    n = NORMED[p][1]
                    act.wait_ge(slab_done, S_MIX + 4 * p + 4)
                    back = [q for q in NORMED if q < p and (q - p) % 2 == 0]
                    if back:
                        act.wait_ge(*pe_out.after("pstat", back[-1]))
                    fn(u(SQ + (p % 2) * 512, P, n * S), acc(G_MIX + p)[:, 0:n * S], ACT.Square).then_inc(*act_out.mark("psq", p))
                q = p - 1
                round_upto(S_MIX + 4 * p + 7)
                if q in NORMED:
                    n = NORMED[q][1]
                    act.wait_ge(*pe_out.after("pstat", q))
                    back = [r for r in NORMED if r < q and (r - q) % 2 == 0]
                    chained(fn(u(LN + (q % 2) * 512, P, n * S), ps[:, 5, 0:n * S], ACT.Ln, bias=eps, scale=1.0 / DH), "pln", q)
                    if back:
                        act.wait_ge(*vec_out.after("qk", back[-1]))
                    fn(u(RS + (q % 2) * 512, P, n * S), u(LN + (q % 2) * 512, P, n * S), ACT.Exp, scale=-0.5).then_inc(*act_out.mark("prs", q))
                if q in VALUES:
                    v0, n = VALUES[q]
                    act.wait_ge(*pe_out.after("vt", q))
                    for c in range(n):
                        last = fn(vn[:, :, v0 + c, :], ps[:, 7, c * S:(c + 1) * S].rearrange("p (t c) -> p t c", t=TT), ACT.Copy)
                    last.then_inc(*act_out.mark("vn", q))
            sg, gg = S_MIX + 4 * PROJ, G_MIX + PROJ
            sA = sg + 12
            act.wait_ge(slab_done, sg + 4)
            fn(u(CTMP, 36, S), acc(gg)[0:36, 0:S], ACT.Exp, scale=-1.0).then_inc(*act_out.mark("cgate"))
            round_upto(sA + 2)
            act.wait_ge(slab_done, sA)
            fn(u(CHID, P, 120), ps[:, 4, 0:120], ACT.Silu).then_inc(*act_out.mark("chid"))
            act.wait_ge(*pe_out.after("gn"))
            fn(gn[:, :, :], ps[:, 7, 0:72].rearrange("p (t c) -> p t c", t=TT), ACT.Copy).then_inc(*act_out.mark("gn"))
            act.wait_ge(*pe_out.after("kcvc"))
            fn(vc[0:NCMP, :, :], ps[0:NCMP, 6, 128:256].rearrange("p (g d) -> p g d", g=2), ACT.Copy).then_inc(*act_out.mark("vc"))
            fn(kcs[:, 0, :], ps[:, 6, 64:64 + NCMP], ACT.Square).then_inc(*act_out.mark("kcsq"))
            act.wait_ge(*pe_out.after("kcstat"))
            chained(fn(kcs[:, 1, :], ps[:, 5, 0:NCMP], ACT.Ln, bias=eps, scale=1.0 / DH), "kcln")
            fn(kcs[:, 2, :], kcs[:, 1, :], ACT.Exp, scale=-0.5).then_inc(*act_out.mark("kcrs"))

            def exps(un):
                act.wait_ge(*biased.after(un["key"]))
                for i, sm in enumerate(un["softmax"]):
                    last = fn(un["E"][:, un["e"], sm["col"]:sm["col"] + sm["n"]], un["E"][:, un["e"], sm["col"]:sm["col"] + sm["n"]],
                              ACT.Exp, bias=negmax[:, un["e"], i:i + 1], accum_out=den[:, un["e"], i:i + 1])
                last.then_inc(*expd.mark(un["key"]))

            def pt_copies(un):
                act.wait_ge(*ptr.after(un["key"]))
                if un["prev"] is not None:
                    act.wait_ge(*pv.after(un["prev"]))
                full, pT = sum(b["n"] == P for b in un["blocks"]), un["pT"]
                last = fn(pT[:, 0:4 * P], ps[:, 1, :], ACT.Copy)
                if full > 4:
                    w = min(full, 8) - 4
                    last = fn(pT[:, 4 * P:(4 + w) * P], ps[:, 7, 0:w * P], ACT.Copy)
                if full > 8:
                    last = fn(pT[:, 8 * P:9 * P], ps[:, 3, S:S + P], ACT.Copy)
                if full < len(un["blocks"]):
                    k = len(un["blocks"]) - full
                    last = fn(pT[0:NCMP, full * P:(full + k) * P], ps[0:NCMP, 7, (full - 4) * P:(full - 4 + k) * P], ACT.Copy)
                last.then_inc(*ptc.mark(un["key"]))

            first = units_mix()
            act.wait_ge(*vec_out.after("qk", PROJ - 1))
            act.wait_ge(*vec_out.after("kc"))
            for step in range(len(first) + 1):
                n = sA + 4 * step
                round_upto(n + 2)
                if step == len(first):
                    for k in range(5):
                        if k == 0:
                            act.wait_ge(*scores.after(first[-1]["key"]))
                            act.wait_ge(*o_out.after(first[-3]["key"]))
                        fn(osp[:, 0, 2 * k:2 * k + 2, :], oT[:, 2 * k:2 * k + 2, :], ACT.Copy).then_inc(*rounded.mark("heads", k))
                if step > 0:
                    p = step - 1
                    act.wait_ge(slab_done, n)
                    fn(merged[:, 2 * p:2 * p + 2, :], acc(gg + 1 + p), ACT.Exp, scale=-1.0).then_inc(*act_out.mark("gexp", p))
                if step < len(first):
                    round_upto(n + 3)
                    exps(first[step])
                    round_upto(n + 4)
                if step > 0:
                    pt_copies(first[step - 1])
            n = sA + 4 * GATES
            round_upto(n + 6)
            act.wait_ge(*o_out.after(first[-1]["key"]))
            fn(osp[:, 0, 10:12, :], oT[:, 10:12, :], ACT.Copy).then_inc(*rounded.mark("heads", 5))
            n += 12
            for p in range(8):
                round_upto(n + 2 * p + 4)
                act.wait_ge(evacuated, gg + 1 + GATES + 16 + p + 1)
                fn(hx[:, 0, 2 * p:2 * p + 2, :], merged[:, 2 * p:2 * p + 2, :], ACT.Copy).then_inc(*rounded.mark("merged", p))
            round_upto(n + 16 + 4 * OUTG - 1)

            ffn_act(1, S_F2, G_F2, 2)

            for l in range(2):
                s0, g0 = S_LAY[l], G_LAY[l]
                round_upto(s0 + 2)
                norm_act(3 + l, shift=mod[:, l, 0:16])
                na, ret = units_na(l), units_ret(l)
                for p in range(PIECE + 1):
                    round_upto(s0 + min(4 * p + 2, 4 * PIECE))
                    q = p - 1
                    if q in (8, 9) or q >= 18:
                        act.wait_ge(slab_done, s0 + 4 * q + 4)
                        if q - 1 in (8, 9) or q - 1 >= 18:
                            act.wait_ge(evacuated, g0 + q)
                        fn(u(LT2, P, 512), acc(g0 + q), ACT.Exp, scale=-1.0).then_inc(*act_out.mark("lexp", l, q))
                    round_upto(s0 + min(4 * p + 3, 4 * PIECE))
                    if 6 <= p < 14:
                        exps(na[p - 6])
                    if q in (5, 6) or q in (15, 16):
                        v = q - 1
                        which, c0 = (0 if v < 10 else 1), 2 * (v % 2)
                        act.wait_ge(*pe_out.after("lvt", l, v))
                        for c in range(2):
                            last = fn(lv[:, 2 * which:2 * which + 2, c0 + c, :],
                                      ps[:, 7, c * S:(c + 1) * S].rearrange("p (t c) -> p t c", t=TT), ACT.Copy)
                        last.then_inc(*act_out.mark("lv", l, v))
                    if 6 < p <= 14:
                        round_upto(s0 + 4 * p + 4)
                        pt_copies(na[p - 7])
                    if 18 <= p < 26:
                        hh = p - 18
                        act.wait_ge(*vec_out.after("dexp", l, hh))
                        fn(ebufs["ret"][:, hh % 2, 512:1024], ebufs["ret"][:, hh % 2, 512:1024], ACT.Exp).then_inc(*act_out.mark("dec", l, hh))
                    if 20 <= p < 24:
                        act.wait_ge(*pe_out.after("fy", l, p - 20))
                        fn(fx[:, p - 20, :], ps[:, 7, 0:S], ACT.Copy).then_inc(*act_out.mark("fy", l, p - 20))
                    if p == 22:
                        act.wait_ge(*vec_out.after("centred", l))
                        fn(u(LSQ, P, 1024), u(CY, P, 1024), ACT.Square).then_inc(*act_out.mark("ysq", l))
                    if p == 23:
                        act.wait_ge(*pe_out.after("var", l))
                        chained(fn(lnx, ps[:, 1, 0:S], ACT.Ln, bias=eps, scale=1.0 / 512), "yln", l)
                        fn(rstd[:, :], lnx, ACT.Exp, scale=-0.5).then_inc(*act_out.mark("yrs", l))
                    if p == 24:
                        act.wait_ge(*vec_out.after("yaff", l))
                        fn(u(CY, P, 1024), u(CY, P, 1024), ACT.Silu).then_inc(*act_out.mark("csilu", l))
                act.wait_ge(slab_done, s0 + 4 * PIECE)
                act.wait_ge(*vec_out.after("gated", l, 0))

                def cat_hi(c):
                    fn(hx[:, 0, 4 + 2 * c:6 + 2 * c, :], cT[:, 2 * c:2 * c + 2, :], ACT.Copy).then_inc(*rounded.mark("cat", l, c))

                cat_hi(0)
                cat_hi(1)
                act.wait_ge(*o_out.after("ret", l, 7))
                for c in range(2):
                    fn(u(LSQ + 512 * c, P, 512), u(CT + (4 + 2 * c) * S, P, 512), ACT.Square).then_inc(*act_out.mark("rsq", l, c))
                for c in range(2):
                    act.wait_ge(*pe_out.after("rstat", l, c))
                    chained(fn(u(LT1 + 512 * c, P, 512), ps[:, 6 + c, :], ACT.Ln, bias=eps, scale=1.0 / DH), "rln", l, c)
                    fn(u(LT1 + 512 * c, P, 512), u(LT1 + 512 * c, P, 512), ACT.Exp, scale=-0.5).then_inc(*act_out.mark("rrs", l, c))
                round_upto(s0 + 4 * PIECE + 4)
                for c in range(2):
                    act.wait_ge(*vec_out.after("gated", l, 1 + c))
                    cat_hi(2 + c)
                round_upto(s0 + LAY_SLABS - 1)
            norm_act(5, split=False)

        @block.vector
        def _(dve):
            v = nc.vector

            def chained(ins, *key):
                ins.then_inc(*vec_out.mark(*key))
                dve.wait_ge(*vec_out.after(*key))

            def norm_vec(r, gain, shift=None, split=True):
                dve.wait_ge(*rstd_ready.after(r))
                if r > 0:
                    dve.wait_ge(evacuated, X_READY[r])
                for c in range(DC + (2 if split else 0)):
                    if c < DC:
                        last = v.scalar_tensor_tensor(scr[:, c, :], x[:, c, :], gain[:, c:c + 1], rstd[:, :], ALU.mult, ALU.mult)
                        if split:
                            last.then_inc(*scaled.mark(r, c))
                    if split and c >= 2:
                        m = c - 2
                        dve.wait_ge(*rounded.after(r, m))
                        hi, lo = hx[:, 0, m, :].bitcast(F32), hx[:, 1, m, :]
                        if shift is None:
                            ins = v.tensor_tensor(lo, scr[:, m, :], hi, ALU.subtract)
                        else:
                            ins = v.scalar_tensor_tensor(lo, scr[:, m, :], shift[:, m:m + 1], hi, ALU.add, ALU.subtract)
                        ins.then_inc(*h_ready.mark(r, m))
                if not split:
                    last.then_inc(*h_ready.mark(r))

            def start_squares(r):
                v.memset(squares(r)[1], 0.0)

            def add_squares(r, j, xs, turn=None):
                more = turn or (lambda per: 0)
                t, total = squares(r)
                flat = xs.rearrange("p c s -> p (c s)")
                dve.wait_ge(evacuated, more(4) + (X_READY[r] - 7 + j))
                v.tensor_tensor(t, flat, flat, ALU.mult).then_inc(sq_step, 1)
                dve.wait_ge(sq_step, more(8) + (16 * r + 2 * j + 1))
                v.tensor_tensor(total, total, t, ALU.add).then_inc(sq_step, 1)

            def rest(n):
                return v.tensor_tensor(slab_part(n, 1), stage[:, n % RING, :], slab_part(n, 0).bitcast(F32), ALU.subtract)

            def ada(f, b, q, turn):
                dve.wait_ge(ada_in[q % 2], turn(64) + (768 * f + 32 * b + 16 * (q // 2) + 16))
                w, total = u(ADA_RING, P, 2, KC, W2)[:, q % 2], u(ADA_ACC, P, 2, W2)[:, b % 2, :]
                for kk in range(KC):
                    c = KC * q + kk
                    if c == 0:
                        ins = v.tensor_scalar(total, w[:, 0, :], cact[:, 0:1], None, ALU.mult)
                    else:
                        if kk == 0:
                            dve.wait_ge(ada_quarter, turn(8) + (96 * f + 4 * b + q))
                        else:
                            dve.wait_ge(ada_step, turn(24) + (288 * f + 12 * b + 3 * q + kk))
                        ins = v.scalar_tensor_tensor(total, w[:, kk, :], cact[:, c:c + 1], total, ALU.mult, ALU.add)
                    ins.then_inc(ada_quarter if kk == KC - 1 else ada_step, 1)

            def ffn_vec(f, s0, g0, r, gain):
                norm_vec(r, gain)
                dve.wait_ge(lo_done, nth[s0 + 3])
                with dve.Fori(0, GU_GROUPS // 2) as i:
                    for k in range(2):
                        for q in range(8):
                            n = s0 + 8 * k + 4 + q
                            dve.wait_ge(hi_done, i * 16 + nth[n])
                            rest(n).then_inc(lo_done, 1)
                            if q < 4:
                                ada(f, k, q, lambda per: i * per)
                        dve.wait_ge(slab_done, i * 16 + (s0 + 8 * k + 8))
                        dve.wait_ge(silu_done, i * 2 + (GU_GROUPS * f + k + 1))
                        act_t = u(FTMP, P, 512)
                        v.tensor_tensor(act_t, acc(g0 + k, 1), u(SILU + 512 * k, P, 512), ALU.mult).then_inc(evacuated, 1)
                        dve.wait_ge(evacuated, i * 2 + (g0 + k + 1))
                        hi = ats[:, 0, bass.ds(i * 1024 + 512 * k, 512)]
                        v.tensor_copy(hi, act_t).then_inc(act_split, 1)
                        dve.wait_ge(act_split, i * 4 + (2 * GU_GROUPS * f + 2 * k + 1))
                        v.tensor_tensor(ats[:, 1, bass.ds(i * 1024 + 512 * k, 512)], act_t, hi.bitcast(F32), ALU.subtract
                                        ).then_inc(act_split, 1)
                s1, g1 = s0 + GU_SLABS, g0 + GU_GROUPS
                for q in range(8):
                    ada(f, 22 + q // 4, q % 4, lambda per: 0)
                    n = s1 + 4 + q
                    dve.wait_ge(hi_done, nth[n])
                    rest(n).then_inc(lo_done, 1)
                start_squares(r + 1)
                with dve.Fori(0, DOWN_GROUPS // 4) as i:
                    for k in range(4):
                        dve.wait_ge(slab_done, i * (4 * DOWN) + (s1 + DOWN * (k + 1)))
                        xs = x[:, bass.ds(i * 8 + 2 * k, 2), :]
                        v.scalar_tensor_tensor(xs, acc(g1 + k).rearrange("p (c s) -> p c s", c=2), 0.5, xs, ALU.mult, ALU.add
                                               ).then_inc(evacuated, 1)
                        add_squares(r + 1, k, xs, lambda per, i=i: i * per)
                dve.wait_ge(ada_red, f + 1)
                chained(v.tensor_tensor(mod[:, f, :], ps[:, 4, 0:48], pcol("b_ada_2", 48 * f, 48), ALU.add), "mod", f)
                chained(v.scalar_tensor_tensor(ascale[:, f, :], mod[:, f, 16:32], 1.0, pcol("norm_g_2", 16 * f, 16), ALU.add, ALU.mult),
                        "ascale", f)

            start_squares(0)
            for g in range(G_LOAD):
                dve.wait_ge(*xt.after(g))
                v.tensor_copy(x[:, 2 * g:2 * g + 2, :], acc(g)).then_inc(evacuated, 1)
                add_squares(0, g, x[:, 2 * g:2 * g + 2, :])
            at = 0
            for t, tile in enumerate(PARAM_TILES):
                n = sum(w for _, w in tile)
                dve.wait_ge(*pt_done.after(len(PARAM_TILES) - 1))
                chained(v.tensor_copy(par[:, at:at + n], ps[:, 6 + t // 4, (t % 4) * P:(t % 4) * P + n]), "par", t)
                at += n
            for q in (0, 2, 4):
                last = v.tensor_scalar(pcol("qk_gain", q), pcol("qk_gain", q), DH ** -0.5, None, ALU.mult)
            last.then_inc(*vec_out.mark("gains"))
            dve.wait_ge(*act_out.after("cact"))
            dve.wait_ge(*act_out.after("lexp"))
            yv, zv, wv = lgt[:, 1, :], lgt[:, 0, :], lgt[:, 2, :]
            chained(v.tensor_scalar(zv, yv, 2.0, None, ALU.add), "l0")
            chained(v.reciprocal(zv, zv), "l1")
            chained(v.tensor_tensor(zv, zv, yv, ALU.mult), "l2")
            chained(v.tensor_tensor(yv, zv, zv, ALU.mult), "l3")
            chained(v.tensor_scalar(wv, yv, 1.0 / 19, 1.0 / 17, ALU.mult, ALU.add), "l4")
            for k in range(15, 0, -2):
                chained(v.tensor_tensor(wv, wv, yv, ALU.mult), "l5", k)
                chained(v.tensor_scalar(wv, wv, 1.0 / k, None, ALU.add), "l6", k)
            chained(v.tensor_tensor(wv, wv, zv, ALU.mult), "l7")
            flat = logit[:, :, :].rearrange("p a b -> p (a b)")
            chained(v.tensor_scalar(flat, flat, 0.0, None, ALU.min), "l8")
            chained(v.scalar_tensor_tensor(flat, wv, -2.0, flat, ALU.mult, ALU.add), "l9")

            ffn_vec(0, S_F1, G_F1, 0, pcol("ffn1_norm", 0, DC))

            norm_vec(1, pcol("mix_norm", 0, DC))
            for p in range(PROJ + 1):
                if p < PROJ:
                    bank = acc(G_MIX + p)
                    dve.wait_ge(slab_done, S_MIX + 4 * p + 4)
                    done = None
                    if p in NORMED:
                        dve.wait_ge(*act_out.after("psq", p))
                    if p in VALUES:
                        n = VALUES[p][1]
                        prev = [q for q in VALUES if q < p and (q - p) % 2 == 0]
                        if prev:
                            dve.wait_ge(*pe_out.after("vt", prev[-1]))
                        done = v.tensor_copy(u(VRAW + (p % 2) * 512, P, n * S), bank[:, (2 - n) * S:2 * S])
                    if p in NORMED:
                        c0, n, row = NORMED[p]
                        done = v.tensor_scalar(qk[:, c0:c0 + n, :], bank[:, 0:n * S].rearrange("p (c s) -> p c s", c=n),
                                               pcol("qk_gain", row), None, ALU.mult)
                    if p == CMP_GROUP:
                        done = v.tensor_copy(u(CRAW, P, 512), bank)
                    done.then_inc(evacuated, 1)
                q = p - 1
                if q in NORMED:
                    c0, n, row = NORMED[q]
                    dve.wait_ge(*act_out.after("prs", q))
                    dve.wait_ge(evacuated, G_MIX + q + 1)
                    v.tensor_tensor(qk[:, c0:c0 + n, :], qk[:, c0:c0 + n, :], u(RS + (q % 2) * 512, P, n, S), ALU.mult
                                    ).then_inc(*vec_out.mark("qk", q))
                if p == CMP_GROUP + 1:
                    dve.wait_ge(evacuated, G_MIX + CMP_GROUP + 1)
                    for kv in range(2):
                        dst = u(CBLK + kv * 480, P, DC, 30)
                        for g in range(2):
                            for e in range(2):
                                at = CRAW + kv * S + e
                                one = U[g * DH:(g + 1) * DH, at:at + 1]
                                src = bass.AP(one.tensor, one.offset, [one.ap[0], [2, DC], [CMP_STRIDE, NCMP]])
                                last = v.tensor_copy(dst[e * DH:(e + 1) * DH, :, g * NCMP:(g + 1) * NCMP], src)
                    chained(last, "craw")
                    for kv in range(2):
                        dst = u(CBLK + kv * 480, P, DC, 30)
                        pos = pcol("cmp_pos", 16 * kv, 16).unsqueeze(2).broadcast_to([P, DC, 30])
                        last = v.tensor_tensor(dst, dst, pos, ALU.add)
                    last.then_inc(*vec_out.mark("cblk"))
            sg, gg = S_MIX + 4 * PROJ, G_MIX + PROJ
            dve.wait_ge(*act_out.after("cgate"))
            ct = u(CTMP, 36, S)
            ins = v.tensor_scalar(ct, ct, 1.0, None, ALU.add)
            ins.then_inc(evacuated, 1)
            dve.wait_ge(evacuated, gg + 1)
            v.reciprocal(ct, ct).then_inc(*vec_out.mark("cgate"))
            dve.wait_ge(*act_out.after("kcrs"))
            v.scalar_tensor_tensor(kc[:, :], ps[:, 6, 64:64 + NCMP], pcol("qk_gain", 5), kcs[:, 2, :], ALU.mult, ALU.mult
                                   ).then_inc(*vec_out.mark("kc"))

            def bias_of(un):
                dve.wait_ge(*scores.after(un["key"]))
                e = un["e"]
                if un["prev2"] is not None:
                    dve.wait_ge(*ptr.after(un["prev2"]))
                if "sink" in un:
                    for at in (P, T1 + S):
                        v.tensor_copy(un["E"][:, e, at:at + 1], sinks[:, un["sink"]:un["sink"] + 1])
                for seg in un["segs"]:
                    sc = ps[:, seg["bank"], seg["col"]:seg["col"] + seg["n"]]
                    dst = un["E"][:, e, seg["ecol"]:seg["ecol"] + seg["n"]]
                    if seg.get("nbias") is not None:
                        last = v.tensor_tensor(dst, sc, seg["nbias"], ALU.add)
                    else:
                        last = v.scalar_tensor_tensor(dst, seg["dist"], -seg["slope"], sc, ALU.mult, ALU.add)
                chained(last, "bias", un["key"])
                for i, sm in enumerate(un["softmax"]):
                    last = v.reduce_max(negmax[:, e, i:i + 1], un["E"][:, e, sm["col"]:sm["col"] + sm["n"]], AXX, negate=True)
                last.then_inc(*biased.mark(un["key"]))

            def normalise(un):
                e, k = un["e"], len(un["softmax"])
                dve.wait_ge(*expd.after(un["key"]))
                for i, sm in enumerate(un["softmax"]):
                    if sm.get("mask") is not None:
                        cols = un["E"][:, e, sm["col"]:sm["col"] + sm["n"]]
                        chained(v.tensor_tensor(cols, cols, sm["mask"], ALU.mult), "msk", un["key"], i)
                        chained(v.reduce_sum(den[:, e, i:i + 1], cols, AXX), "msum", un["key"], i)
                if un.get("gate") is not None:
                    chained(v.tensor_scalar(den[:, e, 0:k], den[:, e, 0:k], 1e-30, None, ALU.max), "dmax", un["key"])
                chained(v.reciprocal(rden[:, e, 0:k], den[:, e, 0:k]), "rden", un["key"])
                if un.get("gate") is not None:
                    gcols = gn[:, :, 3 * un["gate"]:3 * un["gate"] + 3]
                    rv = rden[:, e, 0:6].rearrange("p (t b) -> p t b", t=TT)
                    chained(v.tensor_tensor(rv, rv, gcols, ALU.mult), "rgate", un["key"])
                for i, sm in enumerate(un["softmax"]):
                    cols = un["E"][:, e, sm["col"]:sm["col"] + sm["n"]]
                    last = v.tensor_scalar(cols, cols, rden[:, e, i:i + 1], None, ALU.mult)
                last.then_inc(*probs.mark(un["key"]))

            def head_out(un):
                dve.wait_ge(*pv.after(un["key"]))
                r0 = un["half"] * DH
                v.tensor_copy(un["out"][r0:r0 + DH, :], ps[r0:r0 + DH, 3, 0:S]).then_inc(*o_out.mark(un["key"]))

            first = units_mix()
            dve.wait_ge(*act_out.after("gn"))
            dve.wait_ge(mix_in, MIXC)
            def heads_rest(k):
                dve.wait_ge(*rounded.after("heads", k))
                v.tensor_tensor(osp[:, 1, 2 * k:2 * k + 2, :], oT[:, 2 * k:2 * k + 2, :], osp[:, 0, 2 * k:2 * k + 2, :].bitcast(F32),
                                ALU.subtract).then_inc(*heads_ready.mark(k))

            for step in range(len(first) + 1):
                if step < len(first):
                    bias_of(first[step])
                if step > 1:
                    head_out(first[step - 2])
                if step == len(first):
                    for k in range(5):
                        heads_rest(k)
                if step > 0:
                    p = step - 1
                    dve.wait_ge(*act_out.after("gexp", p))
                    G = merged[:, 2 * p:2 * p + 2, :]
                    v.tensor_scalar(G, G, 1.0, None, ALU.add).then_inc(evacuated, 1)
                    dve.wait_ge(evacuated, gg + 1 + p + 1)
                    v.reciprocal(G, G).then_inc(*vec_out.mark("gate", p))
                if step < len(first):
                    normalise(first[step])
            g, n = gg + 1 + GATES, sg + 12 + 4 * GATES
            dve.wait_ge(*vec_out.after("gate", GATES - 1))

            def merge(br, pair, g):
                G = merged[:, 16 * br + 2 * pair:16 * br + 2 * pair + 2, :]
                product_ = acc(g).rearrange("p (c s) -> p c s", c=2)
                if br == 0:
                    v.tensor_tensor(G, G, product_, ALU.mult).then_inc(evacuated, 1)
                else:
                    chained(v.tensor_tensor(G, G, product_, ALU.mult), "gp", g)
                    M = merged[:, 2 * pair:2 * pair + 2, :]
                    v.tensor_tensor(M, M, G, ALU.add).then_inc(evacuated, 1)

            def merged_rest(p):
                dve.wait_ge(*rounded.after("merged", p))
                v.tensor_tensor(hx[:, 1, 2 * p:2 * p + 2, :], merged[:, 2 * p:2 * p + 2, :], hx[:, 0, 2 * p:2 * p + 2, :].bitcast(F32),
                                ALU.subtract).then_inc(*merged_ready.mark(p))

            for pair in range(8):
                dve.wait_ge(*((slab_done, n + pair // 2 + 1) if pair % 2 else part_done.after(g)))
                merge(0, pair, g)
                g += 1
            n += 4
            head_out(first[-1])
            heads_rest(5)
            for pair in range(8):
                dve.wait_ge(slab_done, n + pair + 1)
                merge(1, pair, g)
                g += 1
            n += 8
            for pair in range(9):
                if pair < 8:
                    dve.wait_ge(slab_done, n + 2 * pair + 2)
                    merge(2, pair, g)
                    g += 1
                if pair > 0:
                    merged_rest(pair - 1)
            n += 16
            start_squares(2)
            for p in range(OUTG):
                dve.wait_ge(slab_done, n + 4 * p + 4)
                X = x[:, 2 * p:2 * p + 2, :]
                v.tensor_tensor(X, X, acc(g + p).rearrange("p (c s) -> p c s", c=2), ALU.add).then_inc(evacuated, 1)
                add_squares(2, p, X)

            ffn_vec(1, S_F2, G_F2, 2, pcol("ffn2_norm", 0, DC))

            for l in range(2):
                s0, g0 = S_LAY[l], G_LAY[l]
                def neighbour_bias(b):
                    dve.wait_ge(*pe_out.after("nb", l, b))
                    dst = nbias.rearrange("p h d k -> p k (h d)")[:, 8 * b:8 * b + 8, :]
                    mask = cst("wmask")[:, 8 * b:8 * b + 8].unsqueeze(2).broadcast_to([P, 8, 48])
                    v.tensor_tensor(dst, ps[:, 6 + b % 2, 0:384].rearrange("p (k x) -> p k x", k=8), mask, ALU.add
                                    ).then_inc(*vec_out.mark("nb", l, b))

                norm_vec(3 + l, ascale[:, l, :], mod[:, l, 0:16])
                v.memset(upad, 0.0).then_inc(*vec_out.mark("pad", l))
                na, ret = units_na(l), units_ret(l)

                def taps(first_tap, last_tap):
                    for at in range(first_tap, min(last_tap, 4 * TAPS)):
                        k, c = at // 4, at % 4
                        col = pcol("conv_w_2a" if l == 0 else "conv_w_2b", at)
                        src = upad[:, c, k:k + S]
                        if k == 0:
                            ins = v.tensor_scalar(cy[:, c, :], src, col, pcol("conv_b_2", 4 * l + c), ALU.mult, ALU.add)
                        else:
                            dve.wait_ge(*vec_out.after("tap", l, c, k - 1))
                            ins = v.scalar_tensor_tensor(cy[:, c, :], src, col, cy[:, c, :], ALU.mult, ALU.add)
                        ins.then_inc(*vec_out.mark("tap", l, c, k))

                for p in range(PIECE + 1):
                    if p == 22:
                        dve.wait_ge(*pe_out.after("mean", l))
                        mu = u(LT2 + 512, P, S)
                        chained(v.tensor_scalar(mu, ps[:, 1, 0:S], 1.0 / 512, None, ALU.mult), "mu", l)
                        mub = u(LT2 + 512, P, 1, S).broadcast_to([P, 4, S])
                        v.tensor_tensor(cy, cy, mub, ALU.subtract).then_inc(*vec_out.mark("centred", l))
                    if 1 <= p <= 4:
                        neighbour_bias(2 * p - 2)
                        neighbour_bias(2 * p - 1)
                    if 6 <= p < 14:
                        bias_of(na[p - 6])
                    if 8 <= p < 16:
                        head_out(na[p - 8])
                    if 18 <= p < 26:
                        hh, un = p - 18, ret[p - 18]
                        tab, lo = un["E"][:, hh % 2, 512:1024], un["E"][:, hh % 2, 0:512]
                        if hh >= 2:
                            dve.wait_ge(*pv.after("ret", l, hh - 2))
                        chained(v.tensor_scalar(lo, cst("dneg"), logit[:, 2 + l, hh:hh + 1], None, ALU.mult), "dn", l, hh)
                        v.scalar_tensor_tensor(tab, cst("dpos"), logit[:, l, hh:hh + 1], lo, ALU.mult, ALU.add
                                               ).then_inc(*vec_out.mark("dexp", l, hh))
                    q = p - 1
                    if 0 <= q < PIECE:
                        bank, k2 = acc(g0 + q), acc(g0 + q).rearrange("p (c s) -> p c s", c=2)
                        c2 = 2 * (q % 2)
                        dve.wait_ge(slab_done, s0 + 4 * q + 4)
                        if q in (0, 1):
                            ins = v.tensor_scalar(lq[:, c2:c2 + 2, :], k2, DH ** -0.5, None, ALU.mult)
                        elif q in (2, 3):
                            ins = v.tensor_copy(lq[:, 4 + c2:6 + c2, :], k2)
                        elif q in (4, 5, 14, 15):
                            ins = v.tensor_copy(u(LT1 + 512 * (q % 2), P, 512), bank)
                        elif q in (6, 7):
                            if q == 6:
                                dve.wait_ge(*vec_out.after("pad", l))
                            ins = v.tensor_copy(upad[:, c2:c2 + 2, TAPS // 2:TAPS // 2 + S], k2)
                        elif q in (8, 9):
                            e = u(LT2, P, 2, S)
                            dve.wait_ge(*act_out.after("lexp", l, q))
                            chained(v.tensor_scalar(e, e, 1.0, None, ALU.add), "s1", l, q)
                            chained(v.reciprocal(e, e), "s2", l, q)
                            mid = upad[:, c2:c2 + 2, TAPS // 2:TAPS // 2 + S]
                            ins = v.tensor_tensor(mid, mid, e, ALU.mult)
                        elif q in (10, 11):
                            ins = v.tensor_scalar(lq[:, 8 + c2:10 + c2, :], k2, DH ** -0.5, None, ALU.mult)
                        elif q in (12, 13):
                            ins = v.tensor_copy(lq[:, 12 + c2:14 + c2, :], k2)
                        elif q in (16, 17):
                            ins = v.tensor_copy(fx[:, c2:c2 + 2, :], k2)
                        else:
                            e = u(LT2, P, 2, S)
                            dve.wait_ge(*act_out.after("lexp", l, q))
                            chained(v.tensor_scalar(e, e, 1.0, None, ALU.add), "s1", l, q)
                            chained(v.reciprocal(e, e), "s2", l, q)
                            ins = v.tensor_tensor(lgate[:, 2 * (q - 18):2 * (q - 18) + 2, :], k2, e, ALU.mult)
                        ins.then_inc(evacuated, 1)
                    q = p - 2
                    if q in (10, 11, 12, 13):
                        c = 8 + 2 * (q - 10)
                        pair = lq[:, c:c + 2, :]
                        cosb = cst("cos").unsqueeze(1).broadcast_to([P, 2, S])
                        sinb = cst("sin").unsqueeze(1).broadcast_to([P, 2, S])
                        t = u(LSQ, P, 2, S)
                        dve.wait_ge(*pe_out.after("rot", l, q))
                        chained(v.tensor_tensor(t, ps[:, 6, :].rearrange("p (c s) -> p c s", c=2), sinb, ALU.mult), "rotp", l, q)
                        chained(v.tensor_tensor(pair, pair, cosb, ALU.mult), "rotc", l, q)
                        v.tensor_tensor(pair, pair, t, ALU.add).then_inc(*vec_out.mark("rotq", l, q))
                    if 6 <= p < 14:
                        normalise(na[p - 6])
                    if 18 <= p < 26:
                        hh = p - 18
                        un = ret[hh]
                        dve.wait_ge(*scores.after(un["key"]))
                        dve.wait_ge(*act_out.after("dec", l, hh))
                        E = un["E"][:, hh % 2, 0:512]
                        v.tensor_tensor(E.rearrange("p (c s) -> p c s", c=2), ps[:, 4:6, 0:S],
                                        un["E"][:, hh % 2, 512:1024].rearrange("p (c s) -> p c s", c=2), ALU.mult
                                        ).then_inc(*biased.mark(un["key"]))
                    if 19 <= p < 27:
                        head_out(ret[p - 19])

                    if 19 <= p < 23:
                        c = p - 19
                        dve.wait_ge(*pe_out.after("fp", l, c))
                        if c > 0:
                            dve.wait_ge(*pe_out.after("fy", l, c - 1))
                        v.tensor_copy(u(LT1, P, 512), ps[:, 6, :]).then_inc(*vec_out.mark("fp", l, c))
                    if TAP0 <= p:
                        if p == TAP0:
                            dve.wait_ge(evacuated, g0 + 10)
                        taps((p - TAP0) * TAPN, (p - TAP0 + 1) * TAPN)
                    if p == 23:
                        dve.wait_ge(*act_out.after("yrs", l))
                        for c in range(4):
                            last = v.scalar_tensor_tensor(cy[:, c, :], cy[:, c, :], pcol("conv_ln_g_2", 4 * l + c), rstd[:, :],
                                                          ALU.mult, ALU.mult)
                        chained(last, "yg", l)
                        for c in range(4):
                            last = v.tensor_scalar(cy[:, c, :], cy[:, c, :], pcol("conv_ln_b_2", 4 * l + c), None, ALU.add)
                        last.then_inc(*vec_out.mark("yaff", l))
                    if p == 24:
                        v.tensor_tensor(cT[:, 0:4, :], cT[:, 0:4, :], lgate[:, 4:8, :], ALU.mult).then_inc(*vec_out.mark("gated", l, 0))

                def cat_lo(c):
                    dve.wait_ge(*rounded.after("cat", l, c))
                    o = slice(4 + 2 * c, 6 + 2 * c)
                    return v.tensor_tensor(hx[:, 1, o, :], cT[:, 2 * c:2 * c + 2, :], hx[:, 0, o, :].bitcast(F32), ALU.subtract)

                def gated_product(k):
                    g, n, chunk = g0 + PIECE + k, s0 + 4 * PIECE + k, (0, 2, 12, 14)[k]
                    gated, o = u(GATED + 512 * k, P, 2, S), slice(chunk, chunk + 2)
                    dve.wait_ge(slab_done, n + 1)
                    v.tensor_tensor(gated, acc(g).rearrange("p (c s) -> p c s", c=2), lgate[:, o, :], ALU.mult).then_inc(evacuated, 1)
                    dve.wait_ge(evacuated, g + 1)
                    chained(v.tensor_copy(hx[:, 0, o, :], gated), "ghi", l, k)
                    return v.tensor_tensor(hx[:, 1, o, :], gated, hx[:, 0, o, :].bitcast(F32), ALU.subtract)

                cat_lo(0)
                cat_lo(1)
                gated_product(0)
                gated_product(1).then_inc(*h_ready.mark("cat", l, 0))
                for c in range(2):
                    dve.wait_ge(*act_out.after("rrs", l, c))
                    o = cT[:, 4 + 2 * c:6 + 2 * c, :]
                    chained(v.tensor_tensor(o, o, u(LT1 + 512 * c, P, 2, S), ALU.mult), "rn", l, c)
                    v.tensor_tensor(o, o, lgate[:, 8 + 2 * c:10 + 2 * c, :], ALU.mult).then_inc(*vec_out.mark("gated", l, 1 + c))
                cat_lo(2)
                cat_lo(3).then_inc(*h_ready.mark("cat", l, 1))
                gated_product(2)
                gated_product(3).then_inc(*h_ready.mark("cat", l, 2))
                g, n = g0 + PIECE + 4, s0 + 4 * PIECE + 4
                start_squares(4 + l)
                for p in range(OUTG):
                    dve.wait_ge(slab_done, n + 4 * p + 4)
                    v.scalar_tensor_tensor(x[:, 2 * p, :], acc(g + p)[:, 0:S], mod[:, l, 32 + 2 * p:33 + 2 * p], x[:, 2 * p, :],
                                           ALU.mult, ALU.add)
                    v.scalar_tensor_tensor(x[:, 2 * p + 1, :], acc(g + p)[:, S:2 * S], mod[:, l, 33 + 2 * p:34 + 2 * p],
                                           x[:, 2 * p + 1, :], ALU.mult, ALU.add).then_inc(evacuated, 1)
                    add_squares(4 + l, p, x[:, 2 * p:2 * p + 2, :])
            norm_vec(5, pcol("final_g_2", 0, DC), split=False)
            for i in range(8):
                T, c4 = i // 4, i % 4
                dve.wait_ge(*pe_out.after("res", i))
                last = v.tensor_copy(u(RES, P, TT, D)[:, T, c4 * 512:(c4 + 1) * 512], ps[:, i % 2, :])
                last.then_inc(*vec_out.mark("res", i))


NAMES = ["x", "ffn1_norm", "ffn1_w_gu", "ffn1_w_down", "mix_norm", "w_in", "qk_gain", "sinks", "cmp_pos", "cmp_w1",
         "cmp_w2", "w_branch_a", "w_branch_b", "w_branch_c", "w_out", "ffn2_norm", "ffn2_w_gu", "ffn2_w_down", "c_2",
         "norm_g_2", "w_ada_2", "b_ada_2", "w_in_2", "w_fft_2", "na_rel_bias_2", "ret_logit_fwd_2",
         "ret_logit_bwd_2", "conv_w_2", "conv_b_2", "conv_ln_g_2", "conv_ln_b_2", "conv_w_pw_2", "w_out_2", "final_g_2"]


def program(nc, shapes, marks, final):
    a = {n: nc.dram_tensor(f"in_{n}", shapes[n], F32, kind="ExternalInput").ap() for n in NAMES}
    const = nc.dram_tensor("in_constants", (P, CONST_COLS), F32, kind="ExternalInput").ap()
    out = nc.dram_tensor("out", (1, S, D), F32, kind="ExternalOutput").ap()
    build(nc, a, out, const, marks, final)


def kernel(**inputs):
    import concourse.bacc as bacc
    from concourse.bass_utils import run_bass_kernel_spmd
    arrays = {f"in_{n}": np.ascontiguousarray(inputs[n]) for n in NAMES}
    arrays["in_constants"] = constant_table()
    shapes = {n: arrays[f"in_{n}"].shape for n in NAMES}
    marks = {}
    program(bacc.Bacc("TRN2", target_bir_lowering=False, num_devices=1), shapes, marks, False)
    nc = bacc.Bacc("TRN2", target_bir_lowering=False, num_devices=1)
    program(nc, shapes, marks, True)
    r = run_bass_kernel_spmd(nc, [arrays], core_ids=[0])
    return r.results[0]["out"]
```
